# Optimizing a Trainium2 kernel written in Bass

```python
import math
import jax, jax.numpy as jnp
from jax import lax
import numpy as np

D_MODEL = 1024
BATCH = 1
SEQ = 512
DEPTH = 2

N_MIXERS = 2
RMS_EPS = 1e-6
NEG_INF = -1e30
A_HEADS = 16
A_KV_HEADS = 4
A_HEAD_DIM = D_MODEL // A_HEADS
A_WINDOW = 128
A_BLOCK = 128
A_IN = (A_HEADS + 2 * A_KV_HEADS) * A_HEAD_DIM
B_HEADS = 8
B_HEAD_DIM = D_MODEL // B_HEADS
B_CONV = 4
B_CHUNK = 64
B_IN = 4 * D_MODEL + 4 * B_HEADS
N_GROUPS = 4
EXPERTS_PER_GROUP = 8
N_EXPERTS = N_GROUPS * EXPERTS_PER_GROUP
TOP_K = 2
D_EXPERT = D_MODEL // 4

kernel_name = "hybrid_swa_gdn_hmoe_encoder"

def rmsnorm(x, g):
    xf = x.astype(jnp.float32)
    y = xf * lax.rsqrt(jnp.mean(xf * xf, axis=-1, keepdims=True) + RMS_EPS) * g.astype(jnp.float32)
    return y.astype(x.dtype)

def l2norm(x):
    return x * lax.rsqrt(jnp.sum(x * x, axis=-1, keepdims=True) + RMS_EPS)

def alibi_slopes(n_heads):
    return np.array([2.0 ** (-8.0 * (h + 1) / n_heads) for h in range(n_heads)], np.float32)

def windowed_attention(h, w_in, q_gain, k_gain, sink, w_out):
    B, S, _ = h.shape
    H, G, dh, BLK = A_HEADS, A_KV_HEADS, A_HEAD_DIM, A_BLOCK
    R = H // G
    nb = S // BLK
    proj = h @ w_in
    q, k, v = jnp.split(proj, [H * dh, (H + G) * dh], axis=-1)
    q = rmsnorm(q.reshape(B, S, H, dh), q_gain)
    k = rmsnorm(k.reshape(B, S, G, dh), k_gain)
    v = v.reshape(B, S, G, dh)
    qb = q.reshape(B, nb, BLK, G, R, dh)
    pad = ((0, 0), (BLK, BLK), (0, 0), (0, 0))
    kp = jnp.pad(k, pad).reshape(B, nb + 2, BLK, G, dh)
    vp = jnp.pad(v, pad).reshape(B, nb + 2, BLK, G, dh)
    kw = jnp.concatenate([kp[:, :-2], kp[:, 1:-1], kp[:, 2:]], axis=2)
    vw = jnp.concatenate([vp[:, :-2], vp[:, 1:-1], vp[:, 2:]], axis=2)
    scores = jnp.einsum('bnqgrd,bnkgd->bngrqk', qb, kw,
                        preferred_element_type=jnp.float32) * (dh ** -0.5)
    qi = np.arange(BLK)
    kj = np.arange(3 * BLK)
    dist = np.abs(BLK + qi[:, None] - kj[None, :]).astype(np.float32)
    s_abs = (np.arange(nb)[:, None] - 1) * BLK + kj[None, :]
    mask = (dist <= A_WINDOW)[None] & ((s_abs >= 0) & (s_abs < S))[:, None, :]
    slopes = alibi_slopes(H).reshape(G, R)
    alibi = -slopes[:, :, None, None] * dist[None, None]
    scores = jnp.where(mask[None, :, None, None], scores + alibi[None, None], NEG_INF)
    sink_b = sink.astype(jnp.float32).reshape(1, 1, G, R, 1, 1)
    m = jnp.maximum(jnp.max(scores, axis=-1, keepdims=True), sink_b)
    p = jnp.exp(scores - m)
    attn = p / (jnp.sum(p, axis=-1, keepdims=True) + jnp.exp(sink_b - m))
    out = jnp.einsum('bngrqk,bnkgd->bnqgrd', attn.astype(vw.dtype), vw)
    return out.reshape(B, S, H * dh) @ w_out

def short_conv(u, w):
    K, C = w.shape
    return lax.conv_general_dilated(u, w[:, None, :].astype(u.dtype), window_strides=(1,),
                                    padding=[(K // 2, K - 1 - K // 2)],
                                    dimension_numbers=('NWC', 'WIO', 'NWC'),
                                    feature_group_count=C)

def gated_delta_chunked(q, k, v, g, beta):
    B, H, S, dk = q.shape
    dv = v.shape[-1]
    C = B_CHUNK
    nc = S // C
    q = q * (dk ** -0.5)
    q, k, v = (t.reshape(B, H, nc, C, t.shape[-1]) for t in (q, k, v))
    g = g.reshape(B, H, nc, C)
    beta = beta.reshape(B, H, nc, C)
    gc = jnp.cumsum(g, axis=-1)
    tril = jnp.tril(jnp.ones((C, C), bool))
    strict = jnp.tril(jnp.ones((C, C), bool), -1)
    diff = gc[..., :, None] - gc[..., None, :]
    decay = jnp.where(tril, jnp.exp(jnp.where(tril, diff, 0.0)), 0.0)
    kb = k * beta[..., None]
    L = jnp.where(strict, jnp.einsum('bhnid,bhnjd->bhnij', kb, k) * decay, 0.0)
    a_mat = L + jnp.eye(C, dtype=L.dtype)
    rhs = jnp.concatenate([v * beta[..., None], kb * jnp.exp(gc)[..., None]], axis=-1)
    sol = lax.linalg.triangular_solve(a_mat, rhs, left_side=True, lower=True, unit_diagonal=True)
    u, w = sol[..., :dv], sol[..., dv:]
    intra = jnp.where(tril, jnp.einsum('bhnid,bhnjd->bhnij', q, k) * decay, 0.0)
    q_dec = q * jnp.exp(gc)[..., None]
    k_dec = k * jnp.exp(gc[..., -1:] - gc)[..., None]
    chunk_decay = jnp.exp(gc[..., -1])

    def step(state, xs):
        q_i, k_i, u_i, w_i, a_i, d_i = xs
        v_new = u_i - jnp.einsum('bhck,bhkv->bhcv', w_i, state)
        o_i = jnp.einsum('bhck,bhkv->bhcv', q_i, state) + jnp.einsum('bhcs,bhsv->bhcv', a_i, v_new)
        state = state * d_i[..., None, None] + jnp.einsum('bhck,bhcv->bhkv', k_i, v_new)
        return state, o_i

    xs = tuple(jnp.moveaxis(t, 2, 0) for t in (q_dec, k_dec, u, w, intra, chunk_decay))
    state0 = jnp.zeros((B, H, dk, dv), jnp.float32)
    _, o = lax.scan(step, state0, xs)
    return jnp.moveaxis(o, 0, 2).reshape(B, H, S, dv)

def gated_deltanet(h, w_in, conv_w, a_log, dt_bias, o_gain, w_out):
    B, S, D = h.shape
    H, dk = B_HEADS, B_HEAD_DIM
    proj = h @ w_in
    qkv, z, a, b = jnp.split(proj, [3 * D, 4 * D, 4 * D + 2 * H], axis=-1)
    qkv = jax.nn.silu(short_conv(qkv, conv_w))
    q, k, v = jnp.split(qkv, 3, axis=-1)

    def heads(t):
        return t.reshape(B, S, H, dk).transpose(0, 2, 1, 3).astype(jnp.float32)

    q, k, v = l2norm(heads(q)), l2norm(heads(k)), heads(v)
    a = a.astype(jnp.float32).reshape(B, S, 2, H).transpose(2, 0, 3, 1)
    b = b.astype(jnp.float32).reshape(B, S, 2, H).transpose(2, 0, 3, 1)
    A = jnp.exp(a_log.astype(jnp.float32))[:, None, :, None]
    g = -A * jax.nn.softplus(a + dt_bias.astype(jnp.float32)[:, None, :, None])
    beta = jax.nn.sigmoid(b)
    o_fwd = gated_delta_chunked(q, k, v, g[0], beta[0])

    def flip(t):
        return jnp.flip(t, axis=2)

    o_bwd = flip(gated_delta_chunked(flip(q), flip(k), flip(v), flip(g[1]), flip(beta[1])))
    o = (o_fwd + o_bwd).transpose(0, 2, 1, 3)
    o = rmsnorm(o, o_gain) * jax.nn.silu(z.reshape(B, S, H, dk).astype(jnp.float32))
    return o.reshape(B, S, D).astype(h.dtype) @ w_out

def hierarchical_moe(h, w_group, b_group, w_expert, b_expert, w_gate, w_up, w_down):
    B, S, D = h.shape
    t = h.reshape(B * S, D)
    g_logits = (t @ w_group).astype(jnp.float32) + b_group.astype(jnp.float32)
    g_prob, g_idx = lax.top_k(jax.nn.softmax(g_logits, axis=-1), 1)
    e_logits = ((t @ w_expert).astype(jnp.float32) + b_expert.astype(jnp.float32)
                ).reshape(-1, N_GROUPS, EXPERTS_PER_GROUP)
    e_sel = jnp.take_along_axis(e_logits, g_idx[:, :, None], axis=1)[:, 0]
    e_prob, e_idx = lax.top_k(jax.nn.softmax(e_sel, axis=-1), TOP_K)
    gate = g_prob * e_prob / jnp.sum(e_prob, axis=-1, keepdims=True)
    expert_id = g_idx * EXPERTS_PER_GROUP + e_idx
    combine = jnp.sum(jax.nn.one_hot(expert_id, N_EXPERTS, dtype=jnp.float32) * gate[..., None], axis=1)
    hid = jax.nn.silu(jnp.einsum('td,edf->tef', t, w_gate)) * jnp.einsum('td,edf->tef', t, w_up)
    hid = hid * combine[..., None].astype(hid.dtype)
    return jnp.einsum('tef,efd->td', hid, w_down).reshape(B, S, D)

def setup_inputs(seed: int = 0) -> dict:
    key = jax.random.key(seed)
    ks = jax.random.split(key, 24)
    n_a = (DEPTH + 1) // 2
    n_b = DEPTH // 2
    f32 = jnp.float32

    def nrm(k, shape, fan_in):
        return jax.random.normal(k, shape, f32) * fan_in ** -0.5

    def gain(k, shape):
        return 1.0 + 0.02 * jax.random.normal(k, shape, f32)

    dt = jnp.exp(jax.random.uniform(ks[12], (n_b, 2, B_HEADS), f32, math.log(1e-3), math.log(1e-1)))
    return {
        "x": jax.random.normal(ks[0], (BATCH, SEQ, D_MODEL), f32),
        "norm_mix": gain(ks[1], (DEPTH, D_MODEL)),
        "norm_ffn": gain(ks[2], (DEPTH, D_MODEL)),
        "attn_w_in": nrm(ks[3], (n_a, D_MODEL, A_IN), D_MODEL),
        "attn_q_gain": gain(ks[4], (n_a, A_HEAD_DIM)),
        "attn_k_gain": gain(ks[5], (n_a, A_HEAD_DIM)),
        "attn_sink": 0.5 * jax.random.normal(ks[6], (n_a, A_HEADS), f32),
        "attn_w_out": nrm(ks[7], (n_a, A_HEADS * A_HEAD_DIM, D_MODEL), A_HEADS * A_HEAD_DIM),
        "gdn_w_in": nrm(ks[8], (n_b, D_MODEL, B_IN), D_MODEL),
        "gdn_conv": nrm(ks[9], (n_b, B_CONV, 3 * D_MODEL), B_CONV),
        "gdn_a_log": jnp.log(jax.random.uniform(ks[10], (n_b, 2, B_HEADS), f32, 1.0, 16.0)),
        "gdn_dt_bias": dt + jnp.log(-jnp.expm1(-dt)),
        "gdn_o_gain": gain(ks[11], (n_b, B_HEAD_DIM)),
        "gdn_w_out": nrm(ks[13], (n_b, D_MODEL, D_MODEL), D_MODEL),
        "moe_w_group": nrm(ks[14], (DEPTH, D_MODEL, N_GROUPS), D_MODEL),
        "moe_b_group": 0.01 * jax.random.normal(ks[15], (DEPTH, N_GROUPS), f32),
        "moe_w_expert": nrm(ks[16], (DEPTH, D_MODEL, N_EXPERTS), D_MODEL),
        "moe_b_expert": 0.01 * jax.random.normal(ks[17], (DEPTH, N_EXPERTS), f32),
        "moe_w_gate": nrm(ks[18], (DEPTH, N_EXPERTS, D_MODEL, D_EXPERT), D_MODEL),
        "moe_w_up": nrm(ks[19], (DEPTH, N_EXPERTS, D_MODEL, D_EXPERT), D_MODEL),
        "moe_w_down": nrm(ks[20], (DEPTH, N_EXPERTS, D_EXPERT, D_MODEL), D_EXPERT),
    }

def reference(x, norm_mix, norm_ffn, attn_w_in, attn_q_gain, attn_k_gain, attn_sink, attn_w_out,
              gdn_w_in, gdn_conv, gdn_a_log, gdn_dt_bias, gdn_o_gain, gdn_w_out,
              moe_w_group, moe_b_group, moe_w_expert, moe_b_expert, moe_w_gate, moe_w_up, moe_w_down):
    for i in range(DEPTH):
        h = rmsnorm(x, norm_mix[i])
        j = i // N_MIXERS
        if i % N_MIXERS == 0:
            x = x + windowed_attention(h, attn_w_in[j], attn_q_gain[j], attn_k_gain[j],
                                       attn_sink[j], attn_w_out[j])
        else:
            x = x + gated_deltanet(h, gdn_w_in[j], gdn_conv[j], gdn_a_log[j], gdn_dt_bias[j],
                                   gdn_o_gain[j], gdn_w_out[j])
        h = rmsnorm(x, norm_ffn[i])
        x = x + hierarchical_moe(h, moe_w_group[i], moe_b_group[i], moe_w_expert[i], moe_b_expert[i],
                                 moe_w_gate[i], moe_w_up[i], moe_w_down[i])
    return x


_drawn_inputs = setup_inputs


def setup_inputs(seed=0):
    import zlib

    import numpy as np

    out = dict(_drawn_inputs(seed))
    spreads = {}
    factors = {'attn_k_gain': 2.669, 'gdn_o_gain': 2.962, 'moe_b_group': 2.872, 'attn_sink': 3.303}
    for name, (base, spread) in spreads.items():
        noise = np.random.default_rng([zlib.crc32(name.encode()), seed]).standard_normal(out[name].shape)
        drawn = base * np.exp(spread * noise) if base else spread * noise
        out[name] = __import__('jax').numpy.asarray(drawn.astype(out[name].dtype))
    for name, factor in factors.items():
        out[name] = (out[name] * factor).astype(out[name].dtype)
    return out
```

```python
import numpy as np
import concourse.bass as bass
from concourse import mybir
from concourse.alu_op_type import AluOpType as ALU
from contextlib import ExitStack

F32 = mybir.dt.float32
F32R = mybir.dt.float32r
I32 = mybir.dt.int32
ACT = mybir.ActivationFunctionType
AX = mybir.AxisListType.X

P = 128
D = 1024
SEQ = 512
TT = SEQ // P
KC = D // P
EPS = 1e-6
PANEL = 512

A_HEADS, A_KV, A_DH = 16, 4, 64
A_IN = (A_HEADS + 2 * A_KV) * A_DH
BAND = 3 * P
SCORES = 12
FAR = 1e32

B_HEADS, B_DK = 8, 128
B_IN = 4 * D + 4 * B_HEADS

GROUPS, PER_GROUP = 4, 8
EXPERTS = GROUPS * PER_GROUP
F = D // 4
FC = F // P
SLOTS = 96
PASSES = -(-SEQ // SLOTS)
ROWS = PASSES * SLOTS
NOBODY = 60000.0
RING = 3
SLOT = (2 * KC * F) + FC * D
REPEL = -1e30


def build(nc, ap, out):
    ctx = ExitStack()
    with ctx:
        def sb(name, shape, dt=F32):
            return ctx.enter_context(nc.sbuf_tensor(name, shape, dt))

        def sem(name):
            return ctx.enter_context(nc.semaphore(name))

        def dram(name, shape):
            return nc.dram_tensor(name, shape, F32, kind="Internal").ap()

        h_rows = [dram(f"h_rows{l}", [SEQ, D]) for l in range(2)]
        tables = [dram(f"slot_table{l}", [EXPERTS * ROWS, 2]) for l in range(2)]
        y_rows = [dram(f"y_rows{l}", [2 * SEQ, D]) for l in range(2)]

        SHARED = (("ht", [P, KC, SEQ]), ("gain", [P, 2, D]), ("ring", [P, RING, SLOT]), ("arena", [P, 18432]))
        with ExitStack() as scope:
            ht, gain, ring, arena = [scope.enter_context(nc.sbuf_tensor(n, shape, F32)) for n, shape in SHARED]
        ht_r, gain_r, ring_r, arena_r = [sb(n + "_r", shape, F32R) for n, shape in SHARED]

        x = sb("x", [P, TT, D])
        hn = sb("hn", [P, TT, D])
        ident = sb("ident", [P, P])
        upper = sb("upper", [P, P])
        ones = sb("ones", [P, P])
        norm_s = sb("norm_s", [P, 3, TT])
        mhalf = sb("mhalf", [P, 32])
        router = sb("router", [P, 2, KC, GROUPS + EXPERTS])
        router_b = sb("router_b", [P, 2, GROUPS + EXPERTS])
        bank = [ctx.enter_context(nc.psum_tensor(f"bank{i}", [P, PANEL], F32)) for i in range(8)]

        def cut(at, *shape):
            size = int(np.prod(shape))
            view = arena[:, at:at + size]
            if len(shape) == 2:
                view = view.rearrange("p (a b) -> p a b", a=shape[0])
            if len(shape) == 3:
                view = view.rearrange("p (a b c) -> p a b c", a=shape[0], b=shape[1])
            return view

        class Layout:
            def __init__(self):
                self.at = 0

            def take(self, *shape):
                view = cut(self.at, *shape)
                self.at += int(np.prod(shape))
                assert self.at <= 18432, self.at
                return view

        gu_full = [sem(f"gu_full{i}") for i in range(RING)]
        up_full = [sem(f"up_full{i}") for i in range(RING)]
        dn_full = [sem(f"dn_full{i}") for i in range(RING)]
        PANELS_A = 5
        MOE_AT = [PANELS_A, PANELS_A + EXPERTS + 10]

        PAIR = 2 * KC * PANEL
        flat_ring = [v[:, :, :].rearrange("p r n -> p (r n)") for v in (ring, ring_r)]
        Q_AT = 17408 - 4096
        gain2 = arena[:, 17408:18432]
        SPLIT = (0, 1, 3, 4)

        def panel(n, high=False, rounded=False):
            at = n % 2 * PAIR + (KC * PANEL if high else 0)
            return flat_ring[rounded][:, at:at + KC * PANEL].rearrange("p (c n) -> p c n", c=KC)

        def ht_high(k, half):
            if k != 3:
                at = (Q_AT - 2048, Q_AT + 2048)[half] if k < 3 else 4096 + half * 2048
                part = arena_r[:, at:at + 2048]
            elif half:
                part = gain_r[:, :, :].rearrange("p a n -> p (a n)")
            else:
                part = flat_ring[True][:, 2 * PAIR:]
            return part.rearrange("p (c n) -> p c n", c=4)

        def ht_parts(k, c, cols):
            return (ht_high(k, c // 4)[:, c % 4, cols], ht_r[:, c, cols])

        def panel_parts(n, c, cols):
            return (panel(n, True, True)[:, c, cols], panel(n, False, True)[:, c, cols])

        def three(pe, dst, a, b, start, stop):
            pe.matmul(dst, a[0], b[0], start=start, stop=False)
            pe.matmul(dst, a[0], b[1], start=False, stop=False)
            return pe.matmul(dst, a[1], b[0], start=False, stop=stop)

        panel_high, panel_low = sem("panel_high"), {"dve": sem("panel_low_dve"), "pool": sem("panel_low_pool")}
        GB = PANELS_A + EXPERTS
        PANELS = list(range(PANELS_A)) + list(range(GB, GB + 10))
        LOW_BY = {n: "pool" if GB <= n < GB + 9 else "dve" for n in PANELS}

        def low_count(n):
            return 4 * sum(1 for m in PANELS if m < n and LOW_BY[m] == LOW_BY[n])

        def split_high(act, n, quarters=range(4)):
            for q in quarters:
                if q == 0:
                    act.wait_ge(gu_full[n % RING], 16 * (n // RING + 1))
                c = slice(2 * q, 2 * q + 2)
                act.copy(panel(n, True, True)[:, c, :], panel(n)[:, c, :]).then_inc(panel_high, 1)

        def split_low(eng, n, quarters=range(4)):
            for q in quarters:
                eng.wait_ge(panel_high, 4 * PANELS.index(n) + q + 1)
                c = slice(2 * q, 2 * q + 2)
                eng.tensor_tensor(panel(n, False, True)[:, c, :], panel(n)[:, c, :],
                                  panel(n, True, True)[:, c, :].bitcast(F32),
                                  ALU.subtract).then_inc(panel_low[LOW_BY[n]], 1)

        def split_done(pe, n, c):
            if c % 2 == 0:
                pe.wait_ge(panel_low[LOW_BY[n]], low_count(n) + c // 2 + 1)

        def gate_up(s):
            return ring[:, s, 0:2 * KC * F].rearrange("p (w c m) -> p w c m", w=2, c=KC)

        def down(s):
            return ring[:, s, 2 * KC * F:SLOT].rearrange("p (m n) -> p m n", m=FC)

        def dn_uses(n):
            l = 0 if n < MOE_AT[1] else 1
            before = sum(1 for k in range(MOE_AT[0], MOE_AT[0] + EXPERTS) if k % RING == n % RING) if l else 0
            return before + sum(1 for k in range(MOE_AT[l], n) if k % RING == n % RING)

        stored_out = sem("result_stored")
        const_in = sem("const_in")
        x_in = [sem(f"x_in{t}") for t in range(TT)]
        gain_in = [sem(f"gain_in{k}") for k in range(4)]
        consts = sem("consts")

        ln = {n: sem(f"norm_{n}") for n in ("squared", "mean", "root", "rows")}
        tp = {n: sem(f"turn_{n}") for n in ("turned", "act", "dve")}
        TPN = [0, 2, 3, 5]
        chain = {e: sem(f"{e}_chain") for e in ("dve", "act", "pool")}
        table_clear = sem("table_clear")

        class Order:
            def __init__(self, eng, s):
                self.eng, self.s, self.n, self.base = eng, s, 0, 0

            def mark(self, ins):
                ins.then_inc(self.s, 1)
                self.n += 1
                return self.base + self.n

            def wait(self, value):
                self.eng.wait_ge(self.s, value)

            def step(self, ins):
                self.wait(self.mark(ins))

        def norm_act(act, k, source):
            for t in range(TT):
                source(act, t)
                act.activation(hn[:, t, :], x[:, t, :], ACT.Square,
                               accum_out=norm_s[:, 0, t:t + 1]).then_inc(ln["squared"], 1)

        def norm_pool(pool, k):
            for t in range(TT):
                pool.wait_ge(ln["mean"], TT * k + t + 1)
                pool.tensor_tensor(norm_s[:, 2, t:t + 1], norm_s[:, 1, t:t + 1], mhalf[:, 0:1],
                                   ALU.pow).then_inc(ln["root"], 1)

        gains = [gain[:, 0, :], gain[:, 1, :], gain2, gain[:, 0, :]]

        def norm_dve(dve, k):
            dve.wait_ge(gain_in[k], 16)
            for t in range(TT):
                dve.wait_ge(ln["squared"], TT * k + t + 1)
                dve.tensor_scalar(norm_s[:, 1, t:t + 1], norm_s[:, 0, t:t + 1], 1.0 / D, EPS,
                                  ALU.mult, ALU.add).then_inc(ln["mean"], 1)
                dve.wait_ge(ln["root"], TT * k + t + 1)
                dve.scalar_tensor_tensor(out=hn[:, t, :], in0=x[:, t, :], scalar=norm_s[:, 2, t:t + 1],
                                         in1=gains[k], op0=ALU.mult, op1=ALU.mult
                                         ).then_inc(ln["rows"], 1)
                if t:
                    turn_dve_one(dve, TPN[k], t - 1)
            turn_dve_one(dve, TPN[k], TT - 1)

        def turn_pe(pe, k, source):
            for t in range(TT):
                source(pe, t)
                for half in range(2):
                    if t >= 2:
                        pe.wait_ge(tp["dve" if half or k in SPLIT else "act"], TT * k + t - 1)
                    b = bank[4 + (2 * t + half) % 4]
                    for j in range(4):
                        last = pe.transpose(b[:, j * P:(j + 1) * P], hn[:, t, half * 4 + j::KC], ident[:, :])
                    last.then_inc(tp["turned"], 1)

        def turn_act(act, k):
            for t in range(TT):
                if k in SPLIT:
                    for half in range(2):
                        act.wait_ge(tp["turned"], 2 * TT * k + 2 * t + 1 + half)
                        last = act.copy(ht_high(k, half)[:, :, t * P:(t + 1) * P],
                                        bank[4 + (2 * t + half) % 4][:, :].rearrange("p (c n) -> p c n", c=4))
                    last.then_inc(tp["act"], 1)
                    continue
                act.wait_ge(tp["turned"], 2 * TT * k + 2 * t + 1)
                act.copy(ht[:, 0:4, t * P:(t + 1) * P],
                         bank[4 + (2 * t) % 4][:, :].rearrange("p (c n) -> p c n", c=4)
                         ).then_inc(tp["act"], 1)

        def turn_dve_one(dve, k, t):
            if k in SPLIT:
                dve.wait_ge(tp["act"], TT * k + t + 1)
                for half in range(2):
                    last = dve.tensor_tensor(ht_r[:, 4 * half:4 * half + 4, t * P:(t + 1) * P],
                                             bank[4 + (2 * t + half) % 4][:, :].rearrange("p (c n) -> p c n", c=4),
                                             ht_high(k, half)[:, :, t * P:(t + 1) * P].bitcast(F32), ALU.subtract)
                last.then_inc(tp["dve"], 1)
                return
            dve.wait_ge(tp["turned"], 2 * TT * k + 2 * t + 2)
            dve.tensor_copy(ht[:, 4:8, t * P:(t + 1) * P],
                            bank[4 + (2 * t + 1) % 4][:, :].rearrange("p (c n) -> p c n", c=4)
                            ).then_inc(tp["dve"], 1)

        def turned(eng, k, t):
            eng.wait_ge(tp["act"], TT * k + t + 1)
            eng.wait_ge(tp["dve"], TT * k + t + 1)

        back = sem("back_sum")

        def project_back_pe(pe, k, n, tpk):
            for t in range(TT):
                turned(pe, tpk, t)
                for half in range(2):
                    u = 2 * t + half
                    if u >= 4:
                        pe.wait_ge(x_half, 2 * TT * k + u - 3)
                    for c in range(KC):
                        if t == 0:
                            split_done(pe, n + half, c)
                        last = three(pe, bank[u % 4][:, :], ht_parts(tpk, c, slice(t * P, (t + 1) * P)),
                                     panel_parts(n + half, c, slice(0, PANEL)), c == 0, c == KC - 1)
                    last.then_inc(back, 1)

        x_half = sem("x_half")

        def project_back_dve(dve, k):
            for t in range(TT):
                for half in range(2):
                    u = 2 * t + half
                    dve.wait_ge(back, 2 * TT * k + u + 1)
                    dst = x[:, t, half * PANEL:(half + 1) * PANEL]
                    dve.tensor_tensor(dst, dst, bank[u % 4][:, :], ALU.add).then_inc(x_half, 1)

        al = Layout()
        v_tok = al.take(TT, A_KV * A_DH)
        at_raw = al.at
        k_raw = al.take(TT, A_KV * A_DH)
        k_two = al.take(TT, A_KV, 2 * A_DH)
        square = cut(17408, 2, PANEL)
        al.at = at_raw
        s_ring = al.take(SCORES, BAND)
        k_t = al.take(A_KV, SEQ)
        dist = al.take(BAND)
        bias = al.take(3, BAND)
        p_t = al.take(3, BAND)
        head_ss = al.take(12, 3, 8)
        top = al.take(2, 4 * A_HEADS)
        row_sum = al.take(3, 4 * A_HEADS)
        sink = al.take(A_HEADS)
        qk_gain = al.take(2)
        assert al.at <= Q_AT - 2048
        q_t = cut(Q_AT, A_HEADS // 2, SEQ)
        slopes = [2.0 ** (-8.0 * (h + 1) / A_HEADS) for h in range(A_HEADS)]

        a = {n: sem("a_" + n) for n in (
            "proj", "proj_free", "squares", "sums", "roots", "unit", "qk_turned", "qk_copied",
            "scores", "biased", "bias", "negmax", "weights", "sink_w", "w_turned", "w_act", "w_dve",
            "values", "heads")}
        IN_ORDER = [2, 0, 1]

        def blocks(n):
            return list(range(max(0, n - 1), min(TT - 1, n + 1) + 1))

        def proj_bank(u):
            return bank[u % 4 if u < 8 else 7]

        def attention_pe(pe):
            def project(i, t):
                    u = 4 * i + t
                    if i == 0:
                        turned(pe, 0, t)
                    if u == 8:
                        pe.wait_ge(a["qk_copied"], 8)
                    if u >= 4:
                        pe.wait_ge(a["proj_free"], u - 3 if u < 9 else u)
                    for c in range(KC):
                        if t == 0:
                            split_done(pe, i, c)
                        last = three(pe, proj_bank(u)[:, :], ht_parts(0, c, slice(t * P, (t + 1) * P)),
                                     panel_parts(i, c, slice(0, PANEL)), c == 0, c == KC - 1)
                    last.then_inc(a["proj"], 1)

            for i in range(2):
                for t in range(TT):
                    project(i, t)
                for m in ([0, 1, 2, 3] if i == 1 else []):
                    turn_qk(pe, m)
            for m in range(4, 8):
                turn_qk(pe, m)
            for h in range(A_HEADS + 3):
                for n in range(TT):
                    u, bs = TT * h + n, blocks(n)
                    if u < TT * A_HEADS:
                        pe.wait_ge(a["qk_copied"], 5 + h // 2)
                        if u >= 3:
                            pe.wait_ge(a["biased"], u - 2)
                        else:
                            pe.wait_ge(a["proj_free"], 8)
                        o = A_DH * (h % 2)
                        pe.matmul(bank[u % 3][:, 0:len(bs) * P], q_t[o:o + A_DH, h // 2, n * P:(n + 1) * P],
                                  k_t[o:o + A_DH, h // 4, bs[0] * P:(bs[-1] + 1) * P],
                                  start=True, stop=True).then_inc(a["scores"], 1)
                    u -= 2 * TT
                    if 0 <= u < TT * A_HEADS:
                        pe.wait_ge(a["weights"], u + 1)
                        if u >= 2:
                            pe.wait_ge(a["w_dve" if u % 2 else "w_act"], u // 2)
                        for j in range(len(bs)):
                            last = pe.transpose(bank[3 + u % 2][:, j * P:(j + 1) * P],
                                                s_ring[:, u % SCORES, j * P:(j + 1) * P], ident[:, :])
                        last.then_inc(a["w_turned"], 1)
                    u -= 2
                    if 0 <= u < TT * A_HEADS:
                        head, m = u // TT, u % TT
                        pe.wait_ge(a["w_dve" if u % 2 else "w_act"], u // 2 + 1)
                        if m == 0 and head >= 2:
                            pe.wait_ge(a["heads"], head - 1)
                        keys = blocks(m)
                        for j, kb in enumerate(keys):
                            last = pe.matmul(bank[5 + head % 2][:, m * A_DH:(m + 1) * A_DH],
                                             p_t[:, u % 3, j * P:(j + 1) * P],
                                             v_tok[:, kb, head // 4 * A_DH:(head // 4 + 1) * A_DH],
                                             start=j == 0, stop=j == len(keys) - 1)
                        last.then_inc(a["values"], 1)
                    if n == 1 and h < 4:
                        project(2, h)
                    if n == 1 and 5 <= h <= 8:
                        turn_qk(pe, 3 + h)

        def qk_bank(m):
            return bank[4 + m % 4 if m < 8 else 7]

        def turn_qk(pe, m):
            pe.wait_ge(a["unit"], 4 if m < 4 else 8 if m < 8 else 12)
            if m >= 4:
                pe.wait_ge(a["qk_copied"], m - 3 if m < 8 else m)
            if m == 8:
                pe.wait_ge(a["proj_free"], 12)
            for t in range(TT):
                src = k_two[:, t, m, :] if m < 4 else hn[:, t, (m - 4) * P:(m - 3) * P]
                last = pe.transpose(qk_bank(m)[:, t * P:(t + 1) * P], src, ident[:, :])
            last.then_inc(a["qk_turned"], 1)

        def attention_act(act):
            def evacuate(i, t):
                    j, u = IN_ORDER[i], 4 * i + t
                    act.wait_ge(a["proj"], u + 1)
                    if u >= 2:
                        act.wait_ge(a["sums"], u - 1)
                    if u == 4:
                        act.wait_ge(tp["turned"], 2 * TT)
                    b = proj_bank(u)
                    if j == 2:
                        act.activation(square[:, u % 2, 0:256], b[:, 0:256], ACT.Square).then_inc(a["squares"], 1)
                        act.copy(k_raw[:, t, :], b[:, 0:256])
                        act.copy(v_tok[:, t, :], b[:, 256:512]).then_inc(a["proj_free"], 1)
                    else:
                        act.activation(square[:, u % 2, :], b[:, :], ACT.Square).then_inc(a["squares"], 1)
                        act.copy(hn[:, t, j * PANEL:(j + 1) * PANEL], b[:, :]).then_inc(a["proj_free"], 1)
                    if i < 2 and t in (1, 2):
                        split_high(act, i + 1, (2 * t - 2, 2 * t - 1))

            for i in range(2):
                for t in range(TT):
                    evacuate(i, t)
            for h in range(A_HEADS + 2):
                for n in range(TT):
                    if h >= 2 and n % 2 == 0:
                        copy_weights(act, h - 2, n, "w_act", act.copy)
                    if h < 4 and n == 2:
                        evacuate(2, h)
                    if 1 <= h <= A_HEADS:
                        if n == 0:
                            act.wait_ge(a["negmax"], h)
                            at = 4 * (h - 1)
                            act.activation(row_sum[:, 1, at:at + 4], top[:, 1, at:at + 4], ACT.Exp,
                                           bias=sink[:, h - 1:h]).then_inc(a["sink_w"], 1)
                        u = TT * (h - 1) + n
                        s = s_ring[:, u % SCORES, 0:len(blocks(n)) * P]
                        act.activation(s, s, ACT.Exp, bias=top[:, 1, u:u + 1],
                                       accum_out=row_sum[:, 0, u:u + 1]).then_inc(a["weights"], 1)
                if 3 <= h < 11:
                    split_high(act, 3 + (h - 3) // 4, ((h - 3) % 4,))

        def copy_weights(eng, h, n, which, copy):
            u = TT * h + n
            width = len(blocks(n)) * P
            eng.wait_ge(a["w_turned"], u + 1)
            if u >= 3:
                eng.wait_ge(a["values"], u - 2)
            copy(p_t[:, u % 3, 0:width], bank[3 + u % 2][:, 0:width]).then_inc(a[which], 1)

        def attention_dve(dve, o):
            o.step(dve.scalar_tensor_tensor(out=dist, in0=dist, scalar=-1.0, in1=dist, op0=ALU.mult, op1=ALU.max))
            unit = 0

            def finish(h):
                g = 4 * h
                dve.wait_ge(a["sink_w"], h + 1)
                dve.wait_ge(a["weights"], g + 4)
                o.step(dve.tensor_tensor(row_sum[:, 2, g:g + 4], row_sum[:, 0, g:g + 4],
                                         row_sum[:, 1, g:g + 4], ALU.add))
                o.step(dve.reciprocal(row_sum[:, 2, g:g + 4], row_sum[:, 2, g:g + 4]))
                dve.wait_ge(a["values"], g + 4)
                dve.tensor_tensor(hn[:, :, h * A_DH:(h + 1) * A_DH],
                                  bank[5 + h % 2][:, 0:TT * A_DH].rearrange("p (n d) -> p n d", n=TT),
                                  row_sum[:, 2, g:g + 4].unsqueeze(2).to_broadcast([P, TT, A_DH]),
                                  ALU.mult).then_inc(a["heads"], 1)

            def squares(i, t):
                    j, u = IN_ORDER[i], 4 * i + t
                    heads = 4 if j == 2 else 8
                    dve.wait_ge(a["squares"], u + 1)
                    o.wait(o.mark(dve.tensor_reduce(head_ss[:, u, 0, 0:heads],
                                      square[:, u % 2, 0:heads * A_DH].rearrange("p (h d) -> p h d", d=A_DH),
                                      AX, ALU.add)))
                    dve.tensor_scalar(head_ss[:, u, 1, 0:heads], head_ss[:, u, 0, 0:heads], 1.0 / A_DH, EPS,
                                      ALU.mult, ALU.add).then_inc(a["sums"], 1)

            for i in range(2):
                j = IN_ORDER[i]
                for t in range(TT):
                    squares(i, t)
                    if t:
                        normalise(dve, 4 * i + t - 1, j, t - 1)
                    if t in (2, 3):
                        split_low(dve, i + 1, (2 * t - 4, 2 * t - 3))
                normalise(dve, 4 * i + TT - 1, j, TT - 1)
                if i == 1:
                    for m in range(8):
                        copy_qk(dve, m)
            for h in range(A_HEADS + 3):
                for n in range(TT):
                    if h < A_HEADS:
                        if n == 0:
                            dve.wait_ge(a["bias"], h + 1)
                        u, w = TT * h + n, len(blocks(n)) * P
                        at = P if n == 0 else 0
                        dve.wait_ge(a["scores"], u + 1)
                        if u >= SCORES:
                            dve.wait_ge(a["w_turned"], u - SCORES + 1)
                        dve.tensor_tensor_reduce(out=s_ring[:, u % SCORES, 0:w], in0=bank[u % 3][:, 0:w],
                                                 in1=bias[:, h % 3, at:at + w], scale=1.0, scalar=-3e38,
                                                 op0=ALU.add, op1=ALU.max,
                                                 accum_out=top[:, 0, u:u + 1]).then_inc(a["biased"], 1)
                    if 2 <= h < A_HEADS + 2 and n % 2:
                        copy_weights(dve, h - 2, n, "w_dve", dve.tensor_copy)
                    if n == 2 and h < 4:
                        squares(2, h)
                    if n == 0 and 1 <= h <= 4:
                        normalise(dve, 7 + h, IN_ORDER[2], h - 1)
                    if n == 1 and 5 <= h <= 8:
                        copy_qk(dve, 3 + h)
                    if n == 2 and h >= 3:
                        finish(h - 3)
                if 3 <= h < 11:
                    split_low(dve, 3 + (h - 3) // 4, ((h - 3) % 4,))
                if h < A_HEADS:
                    dve.wait_ge(a["biased"], TT * h + TT)
                    dve.tensor_scalar(top[:, 1, 4 * h:4 * h + 4], top[:, 0, 4 * h:4 * h + 4],
                                      sink[:, h:h + 1], -1.0, ALU.max, ALU.mult).then_inc(a["negmax"], 1)
        def normalise(dve, u, j, t):
            dve.wait_ge(a["roots"], u + 1)
            dve.wait_ge(a["proj_free"], u + 1)
            if j == 2:
                r = head_ss[:, u, 2, 0:4].unsqueeze(2).to_broadcast([P, 4, A_DH])
                for two in range(2):
                    last = dve.tensor_tensor(k_two[:, t, :, two * A_DH:(two + 1) * A_DH],
                                             k_raw[:, t, :].rearrange("p (h d) -> p h d", d=A_DH), r, ALU.mult)
                last.then_inc(a["unit"], 1)
            else:
                q = hn[:, t, j * PANEL:(j + 1) * PANEL].rearrange("p (h d) -> p h d", d=A_DH)
                r = head_ss[:, u, 2, 0:8].unsqueeze(2).to_broadcast([P, 8, A_DH])
                dve.tensor_tensor(q, q, r, ALU.mult).then_inc(a["unit"], 1)

        def copy_qk(dve, m):
            dve.wait_ge(a["qk_turned"], m + 1)
            if m < 4:
                dve.tensor_scalar(k_t[:, m, :], qk_bank(m)[:, :], qk_gain[:, 1:2], None,
                                  ALU.mult).then_inc(a["qk_copied"], 1)
            else:
                dve.tensor_scalar(q_t[:, m - 4, :], qk_bank(m)[:, :], qk_gain[:, 0:1], A_DH ** -0.5,
                                  ALU.mult, ALU.mult).then_inc(a["qk_copied"], 1)

        def attention_pool(pool):
            def root(u):
                heads = 4 if u < 4 else 8
                pool.wait_ge(a["sums"], u + 1)
                pool.tensor_tensor(head_ss[:, u, 2, 0:heads], head_ss[:, u, 1, 0:heads], mhalf[:, 0:heads],
                                   ALU.pow).then_inc(a["roots"], 1)

            for u in range(8):
                root(u)
            for h in range(A_HEADS):
                if h >= 3:
                    pool.wait_ge(a["biased"], TT * (h - 2))
                pool.tensor_scalar(bias[:, h % 3, :], dist, -slopes[h], 0.0, ALU.mult,
                                   ALU.add).then_inc(a["bias"], 1)
                if 2 <= h < 6:
                    root(6 + h)

        DIRS, LEVELS = 2, 7
        MASKS_AT = 17408 - (LEVELS + 1) * DIRS * P
        level = [cut(MASKS_AT + l * DIRS * P, DIRS, P) for l in range(LEVELS)]
        incl = cut(MASKS_AT + LEVELS * DIRS * P, DIRS, P)
        differ = hn[:, 0, 0:P]
        at_least = hn[:, 1, :].rearrange("p (l n) -> p l n", l=LEVELS + 1)
        bits = hn[:, 2, 0:2 * P].bitcast(I32).rearrange("p (w n) -> p w n", w=2)
        mask_bits = sem("mask_bits")

        def incl_of(d):
            return incl[:, d, :]

        def masks_pool(pool, o):
            pool.memset(incl_of(0), 1.0)
            o.step(pool.memset(incl_of(1), 1.0))
            pool.affine_select(out=incl_of(0), in_=incl_of(0), compare_op=ALU.is_ge, fill=0.0, base=0,
                               pattern=[[-1, P]], channel_multiplier=1)
            o.step(pool.affine_select(out=incl_of(1), in_=incl_of(1), compare_op=ALU.is_ge, fill=0.0, base=0,
                                      pattern=[[1, P]], channel_multiplier=-1))
            pool.wait_ge(s["stored"], 16 * TT)
            pool.wait_ge(tp["turned"], 2 * TT * 3)
            pool.iota(bits[:, 0, :], [[0, P]], base=0, channel_multiplier=1)
            pool.iota(bits[:, 1, :], [[1, P]], base=0, channel_multiplier=0).then_inc(mask_bits, 1)

        def masks_dve(dve, o):
            dve.wait_ge(mask_bits, 1)
            o.step(dve.tensor_tensor(bits[:, 0, :], bits[:, 0, :], bits[:, 1, :], ALU.bitwise_xor))
            o.step(dve.tensor_copy(differ, bits[:, 0, :]))
            for l in range(LEVELS):
                dve.tensor_scalar(at_least[:, l, :], differ, float(2 ** l), None, ALU.is_ge)
            o.step(dve.memset(at_least[:, LEVELS, :], 0.0))
            for l in range(LEVELS):
                last = dve.tensor_tensor(at_least[:, l, :], at_least[:, l, :], at_least[:, l + 1, :], ALU.subtract)
            o.step(last)
            for l in range(LEVELS):
                for d in range(DIRS):
                    last = dve.tensor_tensor(level[l][:, d, :], at_least[:, l, :], incl_of(d), ALU.mult)
            o.step(last)
            for l in range(LEVELS):
                for d in range(DIRS):
                    last = dve.tensor_tensor(level[l][:, d, :], ident[:, :], level[l][:, d, :], ALU.subtract)
            o.step(last)

        ml = Layout()
        xg = ml.take(RING, D)
        xgt = ml.take(RING, KC, SLOTS)
        hidden = ml.take(RING, FC, SLOTS)
        gated = ml.take(RING, FC * SLOTS)
        y_out = ml.take(RING, D)
        y_at = ml.at
        ml.at += 4 * D
        y_in = [cut(at, 2, D) for at in (y_at, y_at + 2 * D, 0, 2 * D)]
        logits = ml.take(TT, GROUPS + EXPERTS)
        oh_g = ml.take(TT, GROUPS)
        key = ml.take(TT, EXPERTS)
        oh = ml.take(2, TT, EXPERTS)
        oh_sum = ml.take(TT, EXPERTS)
        masked = ml.take(2, TT, EXPERTS)
        tmp = ml.take(TT, EXPERTS)
        stat = ml.take(16, TT)
        g_exp = ml.take(TT, GROUPS)
        revs = ml.take(EXPERTS)
        base = ml.take(EXPERTS)
        payload = ml.take(TT, 2 * 2)
        table_sb = ml.take(SLOTS * 2)
        pos_f = ml.take(2, TT)
        nobody = sb("nobody", [P, EXPERTS * ROWS * 2 // P])
        pos_i = sb("pos_i", [P, 2, TT], I32)
        idx_i = sb("idx_i", [P, 2, EXPERTS], I32)
        idx_st = sb("idx_st", [P, RING, 2], I32)
        most_f = ml.take(1)
        late_f = ml.take(2)
        most_i = sb("most_i", [P, 1], I32)

        late_dma = [sem(f"late_dma{l}") for l in range(2)]
        late_weights = [sem(f"late_weights{l}") for l in range(2)]
        late_step = [sem(f"late_step{l}") for l in range(2)]
        PER = dict(most=1, stored=16 * TT, logits=1, pool_c=1, dve=2, exp_g=1, exp_e=1, onehots=1, ranks=1, pos=1,
                   table_in=16 * 2 * TT, table_sb=16, table_t=1, idx=1, combined=TT, y_sum=2 * EXPERTS)
        PER.update({n: EXPERTS for n in ("st", "turned", "t_act", "t_dve", "gate", "silu", "up", "hidden",
                                         "y_act", "y_dve")})
        s = {n: sem("moe_" + n) for n in PER}
        xg_full = [sem(f"xg_full{i}") for i in range(RING)]
        y_stored = [sem(f"y_stored{i}") for i in range(RING)]
        y_back = [sem(f"y_back{t}") for t in range(TT)]
        XG0 = [0, 11]

        def slot_uses(l, s):
            return sum(1 for e in range(EXPERTS) if e % RING == s) * l

        def moe_pool(pool, l, o):
            for t in range(TT):
                pool.wait_ge(ln["rows"], TT * (2 * l + 1) + t + 1)
                pool.dma_start(h_rows[l][t * P:(t + 1) * P, :], hn[:, t, :]).then_inc(s["stored"], 16)
            pool.iota(revs, [[-1, EXPERTS]], base=64, channel_multiplier=0,
                      allow_small_or_imprecise_dtypes=True)
            pool.iota(base, [[ROWS, EXPERTS]], base=0, channel_multiplier=0,
                      allow_small_or_imprecise_dtypes=True)
            for k in range(2):
                for w in range(2):
                    pool.iota(payload[:, :, 2 * k + w], [[P, TT]], base=k * w * SEQ, channel_multiplier=1,
                              allow_small_or_imprecise_dtypes=True)
            for i in range(RING):
                last = pool.memset(xg[:, i, :], 0.0)
            last.then_inc(s["pool_c"], 1)
            if l == 0:
                masks_pool(pool, o)
            pool.wait_ge(s["pool_c"], 1 + l * PER["pool_c"])
            pool.wait_ge(s["pos"], 1 + l * PER["pos"])
            pool.wait_ge(table_clear, 32)
            for k in range(2):
                for t in range(TT):
                    pool.indirect_dma_start(
                        out=tables[l], out_offset=bass.IndirectOffsetOnAxis(ap=pos_i[:, k, t:t + 1], axis=0),
                        in_=payload[:, t, 2 * k:2 * k + 2], in_offset=None,
                        bounds_check=EXPERTS * ROWS - 1, oob_is_err=False).then_inc(s["table_in"], 16)
            pool.wait_ge(s["table_in"], 16 * 2 * TT + l * PER["table_in"])
            pool.dma_start(table_sb[0:EXPERTS, :],
                           tables[l].rearrange("(e r) w -> e (r w)", e=EXPERTS)[:, 0:2 * SLOTS]
                           ).then_inc(s["table_sb"], 16)

            def after(e, more):
                return e + 1 + more if isinstance(e, int) else pool.compute_val(e + 1 + more)

            def gather(e, i, it):
                pool.wait_ge(s["idx"], 1 + l * PER["idx"])
                if it is not None:
                    pool.wait_ge(y_stored[i], 16 * (slot_uses(l, i) + it))
                    pool.wait_ge(s["turned"], e - RING + 1 + l * PER["turned"])
                pool.tensor_copy(idx_st[0:SLOTS, i, :].unsqueeze(2), idx_i[0:SLOTS, :, bass.ds(e, 1)]
                                 ).then_inc(s["st"], 1)
                turn_no = after(e, l * EXPERTS)
                pool.wait_ge(s["stored"], 16 * TT + l * PER["stored"])
                pool.wait_ge(s["st"], turn_no)
                pool.indirect_dma_start(
                    out=xg[0:SLOTS, i, :], out_offset=None, in_=h_rows[l],
                    in_offset=bass.IndirectOffsetOnAxis(ap=idx_st[0:SLOTS, i, 0:1], axis=0),
                    bounds_check=SEQ - 1, oob_is_err=False).then_inc(xg_full[i], 16)

            def scatter(e, i):
                turn_no = after(e, l * EXPERTS)
                pool.wait_ge(s["idx"], 1 + l * PER["idx"])
                pool.wait_ge(s["y_act"], turn_no)
                pool.wait_ge(s["y_dve"], turn_no)
                pool.indirect_dma_start(
                    out=y_rows[l], out_offset=bass.IndirectOffsetOnAxis(ap=idx_st[0:SLOTS, i, 1:2], axis=0),
                    in_=y_out[0:SLOTS, i, :], in_offset=None,
                    bounds_check=2 * SEQ - 1, oob_is_err=False).then_inc(y_stored[i], 16)

            for e in range(RING):
                gather(e, e, None)
            scatter(0, 0)
            gather(3, 0, 1)
            scatter(1, 1)
            gather(4, 1, 1)
            scatter(2, 2)
            with pool.Fori(1, 10) as k:
                for i in range(RING):
                    gather(k * RING + i + 2, (i + 2) % RING, k + (i + 2) // RING)
                    scatter(k * RING + i, i)
            for e in (30, 31):
                scatter(e, e % RING)

            def ready():
                pool.memset(xg[:, 0, :], 0.0).then_inc(late_step[l], 1)

            def late(e, j, after):
                after()
                block = tables[l].rearrange("(e b s) w -> e b s w", e=EXPERTS, b=PASSES)
                pool.dma_start(late_f[0:SLOTS, :], block[bass.ds(e, 1), bass.ds(j, 1)].squeeze(0).squeeze(0)
                               ).then_inc(late_dma[l], 16)
                after("indices")
                pool.indirect_dma_start(
                    out=xg[0:SLOTS, 0, :], out_offset=None, in_=h_rows[l],
                    in_offset=bass.IndirectOffsetOnAxis(ap=idx_st[0:SLOTS, 0, 0:1], axis=0),
                    bounds_check=SEQ - 1, oob_is_err=False).then_inc(late_dma[l], 16)
                after("y_copied")
                pool.indirect_dma_start(
                    out=y_rows[l], out_offset=bass.IndirectOffsetOnAxis(ap=idx_st[0:SLOTS, 0, 1:2], axis=0),
                    in_=y_out[0:SLOTS, 0, :], in_offset=None,
                    bounds_check=2 * SEQ - 1, oob_is_err=False).then_inc(late_dma[l], 16)
                after(dma=3)

            late_passes(pool, l, ready, late)

        LATE_DMA, LATE_STEPS, LATE = 16 * 3, 10, EXPERTS * (PASSES - 1)
        STEP = dict(indices=1, turned=2, copied=4, gate_up=5, silu=6, hidden=7, y=8, y_copied=10)

        def late_passes(eng, l, ready, one_pass):
            eng.wait_ge(s["most"], 1 + l)
            most = eng.value_load(most_i[0:1, 0:1], min_val=0, max_val=SEQ)
            with eng.If(most > SLOTS):
                eng.wait_ge(s["y_act"], EXPERTS * (l + 1))
                eng.wait_ge(s["y_dve"], EXPERTS * (l + 1))
                for i in range(RING):
                    eng.wait_ge(y_stored[i], 16 * slot_uses(l + 1, i))
                if ready:
                    ready()
                with eng.Fori(0, EXPERTS) as e:
                    with eng.Fori(1, PASSES) as j:
                        k = e * (PASSES - 1) + j - 1

                        def after(step=None, dma=None, weights=False):
                            if weights:
                                eng.wait_ge(late_weights[l], eng.compute_val((k + 1) * LATE_DMA))
                                return
                            if dma:
                                value = eng.compute_val(k * LATE_DMA + 16 * dma)
                            else:
                                value = eng.compute_val(k * LATE_STEPS + 1 + (STEP[step] if step else 0))
                            eng.wait_ge(s["most"], 1 + l)
                            eng.wait_ge(late_dma[l] if dma else late_step[l], value)
                        one_pass(e, j, after)
                eng.wait_ge(late_step[l], LATE * LATE_STEPS + 1)
                eng.wait_ge(late_dma[l], LATE * LATE_DMA)
                eng.wait_ge(late_weights[l], LATE * LATE_DMA)

        def moe_pe(pe, l):
            n0 = MOE_AT[l]
            pe.wait_ge(const_in, 16 * 13)
            for t in range(TT):
                turned(pe, TPN[2 * l + 1], t)
                for c in range(KC):
                    last = pe.matmul(bank[0][:, t * 36:(t + 1) * 36], ht[:, c, t * P:(t + 1) * P],
                                     router[:, l, c, :], start=c == 0, stop=c == KC - 1)
            last.then_inc(s["logits"], 1)
            pe.wait_ge(s["onehots"], 1 + l * PER["onehots"])
            pe.matmul(bank[1][:, 0:TT * EXPERTS], upper[:, :], oh_sum.rearrange("p t e -> p (t e)"),
                      start=True, stop=False)
            for k in range(TT - 1):
                pe.matmul(bank[1][:, (k + 1) * EXPERTS:TT * EXPERTS].rearrange("p (t e) -> p t e", e=EXPERTS),
                          ones[:, :], oh_sum[:, k:k + 1, :].to_broadcast([P, TT - 1 - k, EXPERTS]),
                          start=False, stop=k == TT - 2)
            for k in range(TT):
                last = pe.matmul(bank[1][:, TT * EXPERTS:(TT + 1) * EXPERTS], ones[:, :], oh_sum[:, k, :],
                                 start=k == 0, stop=k == TT - 1)
            last.then_inc(s["ranks"], 1)
            pe.wait_ge(s["table_sb"], 16 + l * PER["table_sb"])
            for w in range(2):
                last = pe.transpose(bank[2][0:SLOTS, w * EXPERTS:(w + 1) * EXPERTS],
                                    table_sb[0:EXPERTS, w::2], ident[0:EXPERTS, 0:EXPERTS])
            last.then_inc(s["table_t"], 1)

            def turn(e, i, it):
                pe.wait_ge(xg_full[i], 16 * (slot_uses(l, i) + 1) + 16 * it)
                first = isinstance(e, int) and e == 0
                if not first:
                    pe.wait_ge(s["t_act"], e + l * PER["t_act"])
                    pe.wait_ge(s["t_dve"], e + l * PER["t_dve"])
                for half in range(2):
                    for j in range(4):
                        last = pe.transpose(bank[half][:, j * SLOTS:(j + 1) * SLOTS],
                                            xg[0:SLOTS, i, 4 * half + j::KC], ident[0:SLOTS, 0:SLOTS])
                last.then_inc(s["turned"], 1)

            def body(e, i, last_one):
                static = isinstance(e, int)
                slot = (n0 + i) % RING
                turn_no = (n0 + i) // RING
                it = (e - i) // RING if static else itv[0]
                pe.wait_ge(gu_full[slot], 16 * (turn_no + 1) + 16 * it)
                pe.wait_ge(s["t_act"], e + 1 + l * PER["t_act"])
                pe.wait_ge(s["t_dve"], e + 1 + l * PER["t_dve"])
                w = gate_up(slot)
                for which in range(2):
                    if which:
                        pe.wait_ge(up_full[slot], 16 * (dn_uses(n0 + i) + 1) + 16 * it)
                    for m in range(FC):
                        for c in range(KC):
                            last = pe.matmul(bank[2 + which][:, m * SLOTS:(m + 1) * SLOTS],
                                             w[:, which, c, m::FC], xgt[:, i, c, :],
                                             start=c == 0, stop=c == KC - 1)
                    last.then_inc(s["up" if which else "gate"], 1)
                if not last_one:
                    nxt = (i + 1) % RING
                    turn(e + 1, nxt, it if i < RING - 1 else it + 1)
                pe.wait_ge(dn_full[slot], 16 * (dn_uses(n0 + i) + 1) + 16 * it)
                pe.wait_ge(s["hidden"], e + 1 + l * PER["hidden"])
                if not (static and e == 0):
                    pe.wait_ge(s["y_act"], e + l * PER["y_act"])
                    pe.wait_ge(s["y_dve"], e + l * PER["y_dve"])
                d = down(slot)
                for half in range(2):
                    for m in range(FC):
                        last = pe.matmul(bank[4 + half][0:SLOTS, :], hidden[:, i, m, :],
                                         d[:, m, half * PANEL:(half + 1) * PANEL],
                                         start=m == 0, stop=m == FC - 1)
                    last.then_inc(s["y_sum"], 1)

            def late(e, j, after):
                after(dma=2)
                for half in range(2):
                    for c in range(4):
                        last = pe.transpose(bank[half][:, c * SLOTS:(c + 1) * SLOTS],
                                            xg[0:SLOTS, 0, 4 * half + c::KC], ident[0:SLOTS, 0:SLOTS])
                last.then_inc(late_step[l], 1)
                after("copied")
                after(weights=True)
                for which in range(2):
                    for m in range(FC):
                        for c in range(KC):
                            last = pe.matmul(bank[2 + which][:, m * SLOTS:(m + 1) * SLOTS],
                                             gate_up(0)[:, which, c, m::FC], xgt[:, 0, c, :],
                                             start=c == 0, stop=c == KC - 1)
                last.then_inc(late_step[l], 1)
                after("hidden")
                for half in range(2):
                    for m in range(FC):
                        last = pe.matmul(bank[4 + half][0:SLOTS, :], hidden[:, 0, m, :],
                                         down(0)[:, m, half * PANEL:(half + 1) * PANEL],
                                         start=m == 0, stop=m == FC - 1)
                last.then_inc(late_step[l], 1)

            itv = [None]
            turn(0, 0, 0)
            for e in range(RING):
                body(e, e, False)
            with pe.Fori(1, 10) as k:
                itv[0] = k
                for i in range(RING):
                    body(k * RING + i, i, False)
            for e in (30, 31):
                body(e, e % RING, e == 31)
            late_passes(pe, l, None, late)

        def moe_act(act, l):
            act.wait_ge(s["dve"], 1 + l * PER["dve"])
            act.activation(g_exp, g_exp, ACT.Exp).then_inc(s["exp_g"], 1)
            act.wait_ge(s["dve"], 2 + l * PER["dve"])
            act.activation(stat[:, 6, :], stat[:, 5, :], ACT.Exp).then_inc(s["exp_e"], 1)
            act.wait_ge(s["idx"], 1 + l * PER["idx"])

            def take(e, i):
                act.wait_ge(s["turned"], e + 1 + l * PER["turned"])
                act.copy(xgt[:, i, 0:4, :], bank[0][:, 0:4 * SLOTS].rearrange("p (c n) -> p c n", c=4)
                         ).then_inc(s["t_act"], 1)

            def body(e, i, last_one):
                act.wait_ge(s["gate"], e + 1 + l * PER["gate"])
                act.activation(gated[:, i, :], bank[2][:, 0:FC * SLOTS], ACT.Silu).then_inc(s["silu"], 1)
                if not last_one:
                    take(e + 1, (i + 1) % RING)
                act.wait_ge(s["y_sum"], 2 * e + 1 + l * PER["y_sum"])
                it = (e - i) // RING if isinstance(e, int) else itv[0]
                if l or not isinstance(e, int) or e >= RING:
                    act.wait_ge(y_stored[i], 16 * slot_uses(l, i) + 16 * it)
                act.copy(y_out[0:SLOTS, i, 0:PANEL], bank[4][0:SLOTS, :]).then_inc(s["y_act"], 1)

            itv = [None]
            take(0, 0)
            for e in range(RING):
                body(e, e, False)
            with act.Fori(1, 10) as k:
                itv[0] = k
                for i in range(RING):
                    body(k * RING + i, i, False)
            for e in (30, 31):
                body(e, e % RING, e == 31)

            def late(e, j, after):
                after("turned")
                act.copy(xgt[:, 0, 0:4, :], bank[0][:, 0:4 * SLOTS].rearrange("p (c n) -> p c n", c=4)
                         ).then_inc(late_step[l], 1)
                after("gate_up")
                act.activation(gated[:, 0, :], bank[2][:, 0:FC * SLOTS], ACT.Silu).then_inc(late_step[l], 1)
                after("y")
                act.copy(y_out[0:SLOTS, 0, 0:PANEL], bank[4][0:SLOTS, :]).then_inc(late_step[l], 1)

            late_passes(act, l, None, late)
            for i in range(RING):
                act.wait_ge(y_stored[i], 16 * slot_uses(l + 1, i))
            for t in range(TT):
                for k in range(2):
                    r0 = k * SEQ + t * P
                    act.dma_start(y_in[t][:, k, :], y_rows[l][r0:r0 + P, :]).then_inc(y_back[t], 16)

        def moe_dve(dve, l, o):
            lg = logits[:, :, 0:GROUPS]

            def bc(v, n):
                return v.unsqueeze(2).to_broadcast([P, TT, n])

            def first_max(src, n, col, dst):
                o.step(dve.tensor_reduce(stat[:, col, :], src, AX, ALU.max))
                kk = key[:, :, 0:n]
                o.step(dve.tensor_tensor(kk, src, bc(stat[:, col, :], n), ALU.is_equal))
                o.step(dve.tensor_tensor(kk, kk, revs[:, 0:n].unsqueeze(1).to_broadcast([P, TT, n]), ALU.mult))
                o.step(dve.tensor_reduce(stat[:, 15, :], kk, AX, ALU.max))
                o.step(dve.tensor_tensor(dst, kk, bc(stat[:, 15, :], n), ALU.is_equal))

            dve.wait_ge(s["pool_c"], 1 + l * PER["pool_c"])
            dve.wait_ge(s["logits"], 1 + l * PER["logits"])
            o.step(dve.tensor_tensor(logits, bank[0][:, 0:TT * 36].rearrange("p (t n) -> p t n", t=TT),
                                     router_b[:, l, :].unsqueeze(1).to_broadcast([P, TT, 36]), ALU.add))
            first_max(lg, GROUPS, 0, oh_g)
            dve.tensor_tensor(g_exp, lg, bc(stat[:, 0, :], GROUPS), ALU.subtract).then_inc(s["dve"], 1)
            o.step(dve.tensor_scalar(oh_g, oh_g, -1.0, -REPEL, ALU.add, ALU.mult))
            e4 = "p t (g e) -> p t g e"
            o.step(dve.tensor_tensor(masked[:, 0].rearrange(e4, g=GROUPS),
                                     logits[:, :, GROUPS:].rearrange(e4, g=GROUPS),
                                     oh_g.unsqueeze(3).to_broadcast([P, TT, GROUPS, PER_GROUP]), ALU.add))
            first_max(masked[:, 0], EXPERTS, 1, oh[:, 0])
            o.step(dve.scalar_tensor_tensor(out=masked[:, 1], in0=oh[:, 0], scalar=2 * REPEL, in1=masked[:, 0],
                                            op0=ALU.mult, op1=ALU.add))
            first_max(masked[:, 1], EXPERTS, 2, oh[:, 1])
            dve.tensor_tensor(oh_sum, oh[:, 0], oh[:, 1], ALU.add).then_inc(s["onehots"], 1)
            dve.tensor_tensor(stat[:, 5, :], stat[:, 2, :], stat[:, 1, :], ALU.subtract).then_inc(s["dve"], 1)
            dve.wait_ge(s["ranks"], 1 + l * PER["ranks"])
            o.step(dve.tensor_tensor(tmp, bank[1][:, 0:TT * EXPERTS].rearrange("p (t n) -> p t n", t=TT),
                                     base.unsqueeze(1).to_broadcast([P, TT, EXPERTS]), ALU.add))
            o.step(dve.tensor_reduce(most_f, bank[1][:, TT * EXPERTS:(TT + 1) * EXPERTS], AX, ALU.max))
            dve.tensor_copy(most_i[:, :], most_f).then_inc(s["most"], 1)
            for k in range(2):
                o.step(dve.tensor_tensor(key, tmp, oh[:, k], ALU.mult))
                o.step(dve.tensor_reduce(pos_f[:, k, :], key, AX, ALU.add))
            dve.tensor_copy(pos_i[:, :, :], pos_f).then_inc(s["pos"], 1)
            dve.wait_ge(s["exp_g"], 1 + l * PER["exp_g"])
            dve.wait_ge(s["exp_e"], 1 + l * PER["exp_e"])
            o.step(dve.tensor_reduce(stat[:, 7, :], g_exp, AX, ALU.add))
            o.step(dve.tensor_scalar(stat[:, 8, :], stat[:, 6, :], 1.0, None, ALU.add))
            o.step(dve.tensor_tensor(stat[:, 9, :], stat[:, 7, :], stat[:, 8, :], ALU.mult))
            o.step(dve.reciprocal(stat[:, 10, :], stat[:, 9, :]))
            o.step(dve.tensor_tensor(stat[:, 11, :], stat[:, 10, :], stat[:, 6, :], ALU.mult))
            if l == 0:
                masks_dve(dve, o)
            dve.wait_ge(s["table_t"], 1 + l * PER["table_t"])
            dve.tensor_copy(idx_i[0:SLOTS, :, :], bank[2][0:SLOTS, 0:2 * EXPERTS].rearrange(
                "p (w e) -> p w e", w=2)).then_inc(s["idx"], 1)

            def take(e, i):
                dve.wait_ge(s["turned"], e + 1 + l * PER["turned"])
                dve.tensor_copy(xgt[:, i, 4:8, :], bank[1][:, 0:4 * SLOTS].rearrange("p (c n) -> p c n", c=4)
                                ).then_inc(s["t_dve"], 1)

            def body(e, i, last_one, it):
                dve.wait_ge(s["up"], e + 1 + l * PER["up"])
                dve.wait_ge(s["silu"], e + 1 + l * PER["silu"])
                dve.tensor_tensor(hidden[:, i].rearrange("p m n -> p (m n)"), gated[:, i, :],
                                  bank[3][:, 0:FC * SLOTS], ALU.mult).then_inc(s["hidden"], 1)
                if not last_one:
                    take(e + 1, (i + 1) % RING)
                dve.wait_ge(s["y_sum"], 2 * e + 2 + l * PER["y_sum"])
                if not (isinstance(e, int) and e < RING and l == 0):
                    dve.wait_ge(y_stored[i], 16 * slot_uses(l, i) + 16 * it)
                dve.tensor_copy(y_out[0:SLOTS, i, PANEL:D], bank[5][0:SLOTS, :]).then_inc(s["y_dve"], 1)

            take(0, 0)
            for e in range(RING):
                body(e, e, False, 0)
            with dve.Fori(1, 10) as k:
                for i in range(RING):
                    body(k * RING + i, i, False, k)
            for e in (30, 31):
                body(e, e % RING, e == 31, 10)

            def late(e, j, after):
                after(dma=1)
                dve.tensor_copy(idx_st[0:SLOTS, 0, :], late_f[0:SLOTS, :]).then_inc(late_step[l], 1)
                after("turned")
                dve.tensor_copy(xgt[:, 0, 4:8, :], bank[1][:, 0:4 * SLOTS].rearrange("p (c n) -> p c n", c=4)
                                ).then_inc(late_step[l], 1)
                after("silu")
                dve.tensor_tensor(hidden[:, 0].rearrange("p m n -> p (m n)"), gated[:, 0, :],
                                  bank[3][:, 0:FC * SLOTS], ALU.mult).then_inc(late_step[l], 1)
                after("y")
                dve.tensor_copy(y_out[0:SLOTS, 0, PANEL:D], bank[5][0:SLOTS, :]).then_inc(late_step[l], 1)

            late_passes(dve, l, None, late)
            for t in range(TT):
                dve.wait_ge(y_back[t], 32 * (l + 1))
                o.step(dve.scalar_tensor_tensor(out=x[:, t, :], in0=y_in[t][:, 0, :],
                                                scalar=stat[:, 10, t:t + 1], in1=x[:, t, :],
                                                op0=ALU.mult, op1=ALU.add))
                dve.scalar_tensor_tensor(out=x[:, t, :], in0=y_in[t][:, 1, :],
                                         scalar=stat[:, 11, t:t + 1], in1=x[:, t, :],
                                         op0=ALU.mult, op1=ALU.add).then_inc(s["combined"], 1)

        def rows(w):
            return w.rearrange("(p c) n -> p c n", c=KC)

        HH, HALVES = 4, B_HEADS // 4
        CONV = 4
        CHANNELS = 3 * D // P
        gl = Layout()
        q_tr = gl.take(HH, SEQ)
        k_tr = gl.take(HH, SEQ)
        k_tok = gl.take(HH, TT, P)
        v_tok2 = gl.take(HH, TT, P)
        z_gate = cut(0, TT, D)
        state = gl.take(DIRS, HH * P)
        at0 = gl.at
        buf = {n: [None, None] for n in "EWXLTA"}
        for d in range(DIRS):
            for n in "EWXLTA":
                buf[n][d] = gl.take(HH, P)
        conv_l = Layout()
        conv_l.at = at0
        u_pad = conv_l.take(2, SEQ + CONV)
        conv_acc = conv_l.take(2, SEQ)
        silu_out = conv_l.take(2, SEQ)
        sq = conv_l.take(SEQ)
        q_tok = conv_l.take(2, TT, P)
        assert conv_l.at <= gl.at
        o_square = cut(at0, 2, D)
        assert gl.at <= MASKS_AT
        gl.at = MASKS_AT + (LEVELS + 1) * DIRS * P
        small = {n: gl.take(TT, DIRS * B_HEADS) for n in
                 ("a", "e", "g", "gc", "tot", "eg", "beta", "nbeg", "dl", "kd")}
        qk_ss = gl.take(3, HALVES * 2 * HH, TT)
        o_ss = gl.take(3, TT, B_HEADS)
        conv_w = gl.take(CONV * CHANNELS)
        g_rows = sb("g_rows", [P, 2 * DIRS * B_HEADS + B_DK])
        conv_rows = sb("conv_rows", [CONV * CHANNELS, P])
        ab_w = sb("ab_w", [P, KC, 4 * B_HEADS])
        NB = DIRS * B_HEADS

        g = {n: sem("gdn_" + n) for n in (
            "consts", "ab", "act", "dve", "cum", "conv_w", "pads",
            "proj", "u", "conv", "silu", "ta", "sq", "ss", "rs", "tok", "tc", "kt",
            "prod", "gap", "e", "em", "l", "a", "diag", "at", "lt", "ltc", "x1", "t1", "y", "w", "z", "zc",
            "vb", "ks", "qs", "r", "o1", "v", "vn", "vs", "av", "su", "o2", "s", "zero",
            "zp", "zs", "osq", "oss", "ors", "ready")}

        def chunk(t, d):
            return t if d == 0 else TT - 1 - t

        def by_head(row):
            return row.unsqueeze(1).to_broadcast([P, HH, P])

        def col(name, c, hf, d):
            at = d * B_HEADS + hf * HH
            return small[name][:, c, at:at + HH].unsqueeze(2).to_broadcast([P, HH, P])

        def one(name, c, hf, d, h):
            at = d * B_HEADS + hf * HH + h
            return small[name][:, c, at:at + 1]

        def flat(v):
            return v.rearrange("p a b -> p (a b)")

        def heads_of(b):
            return b[:, :].rearrange("p (h n) -> p h n", h=HH)

        def loads_gdn(act):
            act.dma_start(ab_w[:, :, :], rows(ap["gdn_w_in"][0])[:, :, 4 * D:]).then_inc(g["consts"], 16)
            act.dma_start(g_rows[:, 0:NB], ap["gdn_a_log"].rearrange("a d h -> a (d h)").to_broadcast([P, NB])
                          ).then_inc(g["consts"], 16)
            act.dma_start(g_rows[:, NB:2 * NB], ap["gdn_dt_bias"].rearrange("a d h -> a (d h)").to_broadcast([P, NB])
                          ).then_inc(g["consts"], 16)
            act.dma_start(g_rows[:, 2 * NB:], ap["gdn_o_gain"].to_broadcast([P, B_DK])).then_inc(g["consts"], 16)
            act.dma_start(conv_rows[:, :], ap["gdn_conv"][0].rearrange("k (m p) -> (k m) p", p=P)
                          ).then_inc(g["consts"], 16)

        def units():
            for hf in range(HALVES):
                for w in range(3):
                    for h in range(HH):
                        yield 12 * hf + 4 * w + h, hf, w, h, (8 * hf + 4 * w + h if w < 2 else None)

        UNITS = list(units())
        QUARTERS = [(), (0, 1), (2, 3), ()]

        def gdn_pe(pe):
            pe.wait_ge(g["consts"], 80)
            for t in range(TT):
                turned(pe, 3, t)
                for c in range(KC):
                    for part in range(2):
                        tokens = ht_parts(3, c, slice(t * P, (t + 1) * P))[part].bitcast(F32)
                        last = pe.matmul(bank[0][:, t * 32:(t + 1) * 32], tokens, ab_w[:, c, :],
                                         start=c == 0 and part == 0, stop=c == KC - 1 and part == 1)
            last.then_inc(g["ab"], 1)
            pe.transpose(bank[1][:, 0:CONV * CHANNELS], conv_rows[:, :], ident[0:CONV * CHANNELS, 0:CONV * CHANNELS]
                         ).then_inc(g["conv_w"], 1)
            pe.wait_ge(g["dve"], 2)
            for t in range(TT):
                for d in range(DIRS):
                    pe.matmul(bank[2][:, t * NB + d * B_HEADS:t * NB + (d + 1) * B_HEADS], incl_of(1 - d),
                              small["g"][:, t, d * B_HEADS:(d + 1) * B_HEADS], start=True, stop=True)
                last = pe.matmul(bank[3][:, t * NB:(t + 1) * NB], ones[:, :], small["g"][:, t, :],
                                 start=True, stop=True)
            last.then_inc(g["cum"], 1)
            pe.wait_ge(g["dve"], 4)
            pe.wait_ge(g["pads"], 1)
            for hf in range(HALVES):
                for U, _, w, h, V in UNITS[12 * hf:12 * hf + 12]:
                    n = GB + U // 4
                    if U >= 4:
                        pe.wait_ge(g["u"], U - 3)
                    if h == 0 and w == 0 and hf:
                        pe.wait_ge(g["s"], 8)
                        pe.wait_ge(g["o2"], 8)
                    for c in range(KC):
                        if h == 0:
                            split_done(pe, n, c)
                        last = three(pe, bank[U % 4][:, :], panel_parts(n, c, slice(h * P, (h + 1) * P)),
                                     ht_parts(3, c, slice(0, SEQ)), c == 0, c == KC - 1)
                    last.then_inc(g["proj"], 1)
                    if U % 12 >= 1:
                        to_tokens_pe(pe, UNITS[U - 1])
                    if U % 12 >= 2:
                        to_channels_pe(pe, UNITS[U - 2])
                to_tokens_pe(pe, UNITS[12 * hf + 11])
                for T in range(4 * hf, 4 * hf + 4):
                    scan_pe(pe, T, hf)
            pe.wait_ge(g["s"], 16)
            pe.wait_ge(g["o2"], 16)
            for half in range(2):
                for t in range(TT):
                    u, n = TT * half + t, GB + 6 + half
                    if u >= 4:
                        pe.wait_ge(g["zs"], u - 3)
                    for c in range(KC):
                        if t == 0:
                            split_done(pe, n, c)
                        last = three(pe, bank[u % 4][:, :], ht_parts(3, c, slice(t * P, (t + 1) * P)),
                                     panel_parts(n, c, slice(0, PANEL)), c == 0, c == KC - 1)
                    last.then_inc(g["zp"], 1)

        def to_tokens_pe(pe, unit):
            U = unit[0]
            pe.wait_ge(g["silu"], U + 1)
            if U >= 2:
                pe.wait_ge(g["tok"], U - 1)
            for t in range(TT):
                last = pe.transpose(bank[4 + U % 2][:, t * P:(t + 1) * P], silu_out[:, U % 2, t * P:(t + 1) * P],
                                    ident[:, :])
            last.then_inc(g["ta"], 1)

        def to_channels_pe(pe, unit):
            U, hf, w, h, V = unit
            if V is None:
                return
            pe.wait_ge(g["tok"], U + 1)
            if V >= 2:
                pe.wait_ge(g["kt"], V - 1)
            src = k_tok[:, h] if w else q_tok[:, U % 2]
            for t in range(TT):
                last = pe.transpose(bank[6 + U % 2][:, t * P:(t + 1) * P], src[:, t, :], ident[:, :])
            last.then_inc(g["tc"], 1)

        def scan_pe(pe, T, hf):
            def of(d):
                return 2 * T + d, slice(chunk(T % 4, d) * P, (chunk(T % 4, d) + 1) * P)

            pe.wait_ge(g["kt"], 8 * (hf + 1))
            pe.wait_ge(g["tok"], 12 * (hf + 1))
            for d in range(DIRS):
                n, c = of(d)
                if n >= 2:
                    pe.wait_ge(g["s"], n - 1)
                    pe.wait_ge(g["o2"], n - 1)
                for h in range(HH):
                    o = slice(h * P, (h + 1) * P)
                    pe.matmul(bank[3 * d][:, o], k_tr[:, h, c], k_tr[:, h, c], start=True, stop=True)
                    pe.matmul(bank[3 * d + 1][:, o], q_tr[:, h, c], k_tr[:, h, c], start=True, stop=True)
                    last = pe.matmul(bank[3 * d + 2][:, o],
                                     one("g", chunk(T % 4, d), hf, d, h).to_broadcast([P, P]), incl_of(1 - d),
                                     start=True, stop=True)
                last.then_inc(g["prod"], 1)
            for d in range(DIRS):
                n, c = of(d)
                if T % 4 == 0:
                    pe.wait_ge(g["zero"], 1 + hf)
                if n >= 2:
                    pe.wait_ge(g["r"], n - 1)
                for h in range(HH):
                    o = slice(h * P, (h + 1) * P)
                    last = pe.matmul(bank[6 + d][:, o], k_tr[:, h, c], state[:, d, o], start=True, stop=True)
                last.then_inc(g["ks"], 1)
            for d in range(DIRS):
                n, c = of(d)
                pe.wait_ge(g["gap"], n + 1)
                for h in range(HH):
                    o = slice(h * P, (h + 1) * P)
                    last = pe.matmul(bank[3 * d + 2][:, o], q_tr[:, h, c], state[:, d, o], start=True, stop=True)
                last.then_inc(g["qs"], 1)
            for d in range(DIRS):
                n, c = of(d)
                for ready, b, name, turned_now in (("a", 1, "E", "at"), ("diag", 0, "W", "lt")):
                    pe.wait_ge(g["a"], n + 1)
                    pe.wait_ge(g[ready], n + 1)
                    for h in range(HH):
                        last = pe.transpose(bank[3 * d + b][:, h * P:(h + 1) * P], buf[name][d][:, h, :],
                                            ident[:, :])
                    last.then_inc(g[turned_now], 1)
            for l in range(1, LEVELS):
                for d in range(DIRS):
                    n, c = of(d)
                    if l == 1:
                        pe.wait_ge(g["x1"], n + 1)
                        pe.wait_ge(g["ltc"], 4 * T + 1 + d)
                    else:
                        pe.wait_ge(g["zc"], 22 * T + 4 * (l - 2) + 2 * d + 2)
                    for h in range(HH):
                        last = pe.matmul(bank[3 * d][:, h * P:(h + 1) * P], buf["L"][d][:, h, :],
                                         buf["X"][d][:, h, :], start=True, stop=True)
                    last.then_inc(g["y"], 1)
                for d in range(DIRS):
                    pe.wait_ge(g["w"], 12 * T + 2 * (l - 1) + d + 1)
                    if l == 1:
                        pe.wait_ge(g["o1"], 2 * T + d + 1)
                        pe.wait_ge(g["t1"], 2 * T + d + 1)
                        pe.wait_ge(g["ltc"], 4 * T + 3 + d)
                    for h in range(HH):
                        if l < LEVELS - 1:
                            pe.matmul(bank[3 * d + 1][:, h * P:(h + 1) * P], buf["T"][d][:, h, :],
                                      buf["W"][d][:, h, :], start=True, stop=True)
                        last = pe.matmul(bank[3 * d + 2][:, h * P:(h + 1) * P], buf["W"][d][:, h, :],
                                         buf["T"][d][:, h, :], start=True, stop=True)
                    last.then_inc(g["z"], 1)
            for d in range(DIRS):
                n, c = of(d)
                pe.wait_ge(g["zc"], 22 * T + 20 + d + 1)
                pe.wait_ge(g["r"], n + 1)
                for h in range(HH):
                    last = pe.matmul(bank[3 * d + 2][:, h * P:(h + 1) * P], buf["T"][d][:, h, :],
                                     buf["E"][d][:, h, :], start=True, stop=True)
                last.then_inc(g["v"], 1)
            for d in range(DIRS):
                n, c = of(d)
                pe.wait_ge(g["o1"], n + 1)
                pe.wait_ge(g["vn"], n + 1)
                for h in range(HH):
                    last = pe.matmul(bank[3 * d + 1][:, h * P:(h + 1) * P], buf["A"][d][:, h, :],
                                     buf["W"][d][:, h, :], start=True, stop=True)
                last.then_inc(g["av"], 1)
                pe.wait_ge(g["vs"], n + 1)
                for h in range(HH):
                    last = pe.matmul(bank[3 * d][:, h * P:(h + 1) * P], k_tok[:, h, chunk(T % 4, d), :],
                                     buf["X"][d][:, h, :], start=True, stop=True)
                last.then_inc(g["su"], 1)

        def gdn_act(act):
            act.wait_ge(g["consts"], 80)
            act.activation(g_rows[:, 0:NB], g_rows[:, 0:NB], ACT.Exp).then_inc(g["act"], 1)
            act.wait_ge(g["dve"], 1)
            act.activation(flat(small["e"]), flat(small["e"]), ACT.Exp)
            act.activation(flat(small["beta"]), flat(small["beta"]), ACT.Exp, scale=-1.0).then_inc(g["act"], 1)
            act.wait_ge(g["act"], 2)
            act.activation(flat(small["e"]), flat(small["e"]), ACT.Ln, bias=1.0).then_inc(g["act"], 1)
            act.wait_ge(g["dve"], 3)
            act.activation(flat(small["eg"]), flat(small["gc"]), ACT.Exp)
            act.activation(flat(small["dl"]), flat(small["tot"]), ACT.Exp)
            act.activation(flat(small["kd"]), flat(small["kd"]), ACT.Exp).then_inc(g["act"], 1)
            for hf in range(HALVES):
                for unit in UNITS[12 * hf:12 * hf + 12]:
                    U = unit[0]
                    split_high(act, GB + U // 4 + 1, QUARTERS[U % 4])
                    act.wait_ge(g["proj"], U + 1)
                    act.wait_ge(g["pads"], 1 + hf)
                    if U >= 2:
                        act.wait_ge(g["conv"], U - 1)
                    act.copy(u_pad[:, U % 2, 2:2 + SEQ], bank[U % 4][:, :]).then_inc(g["u"], 1)
                    if U % 12 >= 1:
                        square_act(act, UNITS[U - 1])
                    if U % 12 >= 2:
                        channels_act(act, UNITS[U - 2])
                    act.wait_ge(g["conv"], U + 1)
                    if U >= 2:
                        act.wait_ge(g["ta"], U - 1)
                    act.activation(silu_out[:, U % 2, :], conv_acc[:, U % 2, :], ACT.Silu).then_inc(g["silu"], 1)
                for T in range(4 * hf, 4 * hf + 4):
                    scan_act(act, T, hf)
                    if T == 4:
                        split_high(act, GB + 7)
            for half in range(2):
                for t in range(TT):
                    u = TT * half + t
                    act.wait_ge(g["zp"], u + 1)
                    act.activation(z_gate[:, t, half * PANEL:(half + 1) * PANEL], bank[u % 4][:, :], ACT.Silu
                                   ).then_inc(g["zs"], 1)
                    if half == 0:
                        if t >= 2:
                            act.wait_ge(g["oss"], t - 1)
                        act.wait_ge(g["o2"], 16)
                        act.activation(o_square[:, t % 2, :], hn[:, t, :], ACT.Square).then_inc(g["osq"], 1)
                    elif t in (1, 2):
                        split_high(act, GB + 8, (2 * t - 2, 2 * t - 1))

        def square_act(act, unit):
            U, hf, w, h, V = unit
            if V is None:
                return
            act.wait_ge(g["ta"], U + 1)
            if V >= 1:
                act.wait_ge(g["ss"], V)
            act.activation(sq, bank[4 + U % 2][:, :], ACT.Square).then_inc(g["sq"], 1)

        def channels_act(act, unit):
            U, hf, w, h, V = unit
            if V is None:
                return
            act.wait_ge(g["tc"], V + 1)
            act.copy((k_tr if w else q_tr)[:, h, :], bank[6 + U % 2][:, :]).then_inc(g["kt"], 1)

        def scan_act(act, T, hf):
            for d in range(DIRS):
                n = 2 * T + d
                act.wait_ge(g["gap"], n + 1)
                act.activation(flat(buf["E"][d]), flat(buf["E"][d]), ACT.Exp, scale=-1.0).then_inc(g["e"], 1)
            for d in range(DIRS):
                act.wait_ge(g["lt"], 2 * T + d + 1)
                act.copy(flat(buf["L"][d]), bank[3 * d][:, :]).then_inc(g["ltc"], 1)
            for d in range(DIRS):
                act.wait_ge(g["at"], 2 * T + d + 1)
                act.copy(flat(buf["A"][d]), bank[3 * d + 1][:, :]).then_inc(g["ltc"], 1)
            for l in range(1, LEVELS):
                for d in range(DIRS):
                    act.wait_ge(g["z"], 12 * T + 2 * (l - 1) + d + 1)
                    if l < LEVELS - 1:
                        act.copy(flat(buf["X"][d]), bank[3 * d + 1][:, :]).then_inc(g["zc"], 1)
                    act.copy(flat(buf["T"][d]), bank[3 * d + 2][:, :]).then_inc(g["zc"], 1)
            for d in range(DIRS):
                act.wait_ge(g["v"], 2 * T + d + 1)
                act.copy(flat(buf["W"][d]), bank[3 * d + 2][:, :]).then_inc(g["vn"], 1)

        def gdn_pool(pool, o):
            pool.memset(flat(state), 0.0).then_inc(g["zero"], 1)
            for hf in range(HALVES):
                for U, _, w, h, V in UNITS[12 * hf:12 * hf + 12]:
                    split_low(pool, GB + U // 4 + 1, QUARTERS[U % 4])
                    if V is not None:
                        pool.wait_ge(g["ss"], V + 1)
                        pool.tensor_tensor(qk_ss[:, 2, V, :], qk_ss[:, 1, V, :], mhalf[:, 0:TT], ALU.pow
                                           ).then_inc(g["rs"], 1)
                for T in range(4 * hf, 4 * hf + 4):
                    scan_pool(pool, T, hf)
                    if T == 4:
                        split_low(pool, GB + 7)
            for t in range(TT):
                pool.wait_ge(g["oss"], t + 1)
                pool.tensor_tensor(o_ss[:, 2, t, :], o_ss[:, 1, t, :], mhalf[:, 0:B_HEADS], ALU.pow
                                   ).then_inc(g["ors"], 1)
            split_low(pool, GB + 8)

        def scan_pool(pool, T, hf):
            for d in range(DIRS):
                pool.wait_ge(g["l"], 2 * T + d + 1)
                pool.affine_select(out=buf["W"][d], in_=buf["W"][d], compare_op=ALU.not_equal, fill=1.0,
                                   base=0, pattern=[[0, HH], [-1, P]], channel_multiplier=1).then_inc(g["diag"], 1)
            for d in range(DIRS):
                pool.wait_ge(g["ltc"], 4 * T + 1 + d)
                pool.tensor_tensor(buf["T"][d], buf["L"][d], by_head(level[0][:, 1 - d, :]), ALU.mult
                                   ).then_inc(g["t1"], 1)
            for d in range(DIRS):
                pool.wait_ge(g["at"], 2 * T + d + 1)
                pool.tensor_tensor(buf["E"][d], v_tok2[:, :, chunk(T % 4, d), :],
                                   col("beta", chunk(T % 4, d), hf, d), ALU.mult).then_inc(g["vb"], 1)
            for d in range(DIRS):
                pool.wait_ge(g["vn"], 2 * T + d + 1)
                pool.tensor_tensor(buf["X"][d], buf["W"][d], col("kd", chunk(T % 4, d), hf, d), ALU.mult
                                   ).then_inc(g["vs"], 1)

        def gdn_dve(dve, o):
            sm = {n: flat(v) for n, v in small.items()}
            wide = g_rows[:, NB:2 * NB].unsqueeze(1).to_broadcast([P, TT, NB])
            dve.wait_ge(g["consts"], 80)
            dve.wait_ge(g["ab"], 1)
            ab = bank[0][:, 0:TT * 32].rearrange("p (t n) -> p t n", t=TT)
            dve.tensor_copy(small["beta"], ab[:, :, NB:])
            o.step(dve.tensor_tensor(small["a"], ab[:, :, 0:NB], wide, ALU.add))
            dve.scalar_tensor_tensor(out=sm["e"], in0=sm["a"], scalar=-1.0, in1=sm["a"], op0=ALU.mult,
                                     op1=ALU.min).then_inc(g["dve"], 1)
            o.step(dve.tensor_scalar(sm["a"], sm["a"], 0.0, None, ALU.max))
            dve.wait_ge(g["act"], 3)
            o.step(dve.tensor_tensor(sm["g"], sm["a"], sm["e"], ALU.add))
            o.step(dve.tensor_scalar(sm["beta"], sm["beta"], 1.0, None, ALU.add))
            o.step(dve.reciprocal(sm["beta"], sm["beta"]))
            dve.scalar_tensor_tensor(out=small["g"], in0=small["g"], scalar=-1.0,
                                     in1=g_rows[:, 0:NB].unsqueeze(1).to_broadcast([P, TT, NB]),
                                     op0=ALU.mult, op1=ALU.mult).then_inc(g["dve"], 1)
            dve.wait_ge(g["cum"], 1)
            dve.tensor_copy(sm["gc"], bank[2][:, 0:TT * NB])
            o.step(dve.tensor_copy(sm["tot"], bank[3][:, 0:TT * NB]))
            dve.tensor_tensor(sm["kd"], sm["tot"], sm["gc"], ALU.subtract).then_inc(g["dve"], 1)
            dve.wait_ge(g["conv_w"], 1)
            dve.tensor_copy(conv_w, bank[1][:, 0:CONV * CHANNELS]).then_inc(g["dve"], 1)
            dve.wait_ge(g["act"], 4)
            o.step(dve.scalar_tensor_tensor(out=sm["nbeg"], in0=sm["beta"], scalar=-1.0, in1=sm["eg"],
                                            op0=ALU.mult, op1=ALU.mult))
            for hf in range(HALVES):
                if hf:
                    dve.wait_ge(g["su"], 8)
                for i in range(2):
                    dve.memset(u_pad[:, i, 0:2], 0.0)
                    last = dve.memset(u_pad[:, i, 2 + SEQ:CONV + SEQ], 0.0)
                last.then_inc(g["pads"], 1)
                for unit in UNITS[12 * hf:12 * hf + 12]:
                    U, _, w, h, V = unit
                    m = w * B_HEADS + hf * HH + h
                    dve.wait_ge(g["u"], U + 1)
                    dve.wait_ge(g["pads"], 1 + hf)
                    if U >= 2:
                        dve.wait_ge(g["silu"], U - 1)
                    acc = conv_acc[:, U % 2, :]
                    o.step(dve.tensor_scalar(acc, u_pad[:, U % 2, 0:SEQ], conv_w[:, m:m + 1], None, ALU.mult))
                    for k in range(1, CONV):
                        at = k * CHANNELS + m
                        last = dve.scalar_tensor_tensor(out=acc, in0=u_pad[:, U % 2, k:k + SEQ],
                                                        scalar=conv_w[:, at:at + 1], in1=acc,
                                                        op0=ALU.mult, op1=ALU.add)
                        if k < CONV - 1:
                            o.step(last)
                    last.then_inc(g["conv"], 1)
                    if U % 12 >= 1:
                        tokens_dve(dve, o, UNITS[U - 1])
                tokens_dve(dve, o, UNITS[12 * hf + 11])
                if hf:
                    dve.memset(flat(state), 0.0).then_inc(g["zero"], 1)
                for T in range(4 * hf, 4 * hf + 4):
                    scan_dve(dve, T, hf)
            for t in range(TT):
                dve.wait_ge(g["osq"], t + 1)
                o.step(dve.tensor_reduce(o_ss[:, 0, t, :],
                                         o_square[:, t % 2, :].rearrange("p (h n) -> p h n", h=B_HEADS), AX, ALU.add))
                dve.tensor_scalar(o_ss[:, 1, t, :], o_ss[:, 0, t, :], 1.0 / B_DK, EPS, ALU.mult, ALU.add
                                  ).then_inc(g["oss"], 1)
                ot = hn[:, t, :].rearrange("p (h n) -> p h n", h=B_HEADS)
                o.step(dve.tensor_tensor(ot, ot, g_rows[:, 2 * NB:].unsqueeze(1).to_broadcast([P, B_HEADS, B_DK]),
                                         ALU.mult))
                dve.wait_ge(g["ors"], t + 1)
                o.step(dve.tensor_tensor(ot, ot, o_ss[:, 2, t, :].unsqueeze(2).to_broadcast([P, B_HEADS, B_DK]),
                                         ALU.mult))
            for t in range(TT):
                dve.wait_ge(g["zs"], TT + t + 1)
                dve.tensor_tensor(hn[:, t, :], hn[:, t, :], z_gate[:, t, :], ALU.mult).then_inc(g["ready"], 1)

        def tokens_dve(dve, o, unit):
            U, hf, w, h, V = unit
            src = bank[4 + U % 2][:, :].rearrange("p (t n) -> p t n", t=TT)
            if V is None:
                dve.wait_ge(g["ta"], U + 1)
                dve.tensor_copy(v_tok2[:, h], src).then_inc(g["tok"], 1)
                return
            dve.wait_ge(g["sq"], V + 1)
            o.step(dve.tensor_reduce(qk_ss[:, 0, V, :], sq.rearrange("p (t n) -> p t n", t=TT), AX, ALU.add))
            scale = 1.0 if w else float(B_DK)
            dve.tensor_scalar(qk_ss[:, 1, V, :], qk_ss[:, 0, V, :], EPS, scale, ALU.add, ALU.mult
                              ).then_inc(g["ss"], 1)
            dve.wait_ge(g["rs"], V + 1)
            if w == 0 and V % 8 >= 2:
                dve.wait_ge(g["tc"], V - 1)
            dve.tensor_tensor(k_tok[:, h] if w else q_tok[:, U % 2], src,
                              qk_ss[:, 2, V, :].unsqueeze(2).to_broadcast([P, TT, P]), ALU.mult
                              ).then_inc(g["tok"], 1)

        def scan_dve(dve, T, hf):
            for d in range(DIRS):
                dve.wait_ge(g["prod"], 2 * T + d + 1)
                for h in range(HH):
                    last = dve.tensor_scalar(buf["E"][d][:, h, :], bank[3 * d + 2][:, h * P:(h + 1) * P],
                                             one("gc", chunk(T % 4, d), hf, d, h), 0.0, ALU.subtract, ALU.max)
                last.then_inc(g["gap"], 1)
            def masked_decay(d):
                dve.wait_ge(g["e"], 2 * T + d + 1)
                dve.tensor_tensor(buf["E"][d], buf["E"][d], by_head(incl_of(d)), ALU.mult).then_inc(g["em"], 1)

            def make_l(d):
                dve.wait_ge(g["em"], 2 * T + d + 1)
                for h in range(HH):
                    last = dve.scalar_tensor_tensor(out=buf["W"][d][:, h, :], in0=bank[3 * d][:, h * P:(h + 1) * P],
                                                    scalar=one("beta", chunk(T % 4, d), hf, d, h),
                                                    in1=buf["E"][d][:, h, :], op0=ALU.mult, op1=ALU.mult)
                last.then_inc(g["l"], 1)

            def make_a(d):
                dve.wait_ge(g["l"], 2 * T + d + 1)
                dve.tensor_tensor(flat(buf["E"][d]), bank[3 * d + 1][:, :], flat(buf["E"][d]), ALU.mult
                                  ).then_inc(g["a"], 1)

            masked_decay(0)
            make_l(0)
            masked_decay(1)
            make_a(0)
            make_l(1)
            make_a(1)
            for d in range(DIRS):
                n, c = 2 * T + d, chunk(T % 4, d)
                dve.wait_ge(g["diag"], n + 1)
                dve.tensor_tensor(buf["X"][d], buf["W"][d], by_head(level[0][:, d, :]), ALU.mult
                                  ).then_inc(g["x1"], 1)
                if T % 4 >= 2:
                    dve.wait_ge(g["o2"], 2 * T)
                dve.wait_ge(g["qs"], n + 1)
                for h in range(HH):
                    head = hf * HH + h
                    dst = hn[:, c, head * P:(head + 1) * P]
                    src = bank[3 * d + 2][:, h * P:(h + 1) * P]
                    if T % 4 < 2:
                        last = dve.tensor_scalar(dst, src, one("eg", c, hf, d, h), None, ALU.mult)
                    else:
                        last = dve.scalar_tensor_tensor(out=dst, in0=src, scalar=one("eg", c, hf, d, h), in1=dst,
                                                        op0=ALU.mult, op1=ALU.add)
                last.then_inc(g["o1"], 1)
            for l in range(1, LEVELS):
                for d in range(DIRS):
                    dve.wait_ge(g["y"], 12 * T + 2 * (l - 1) + d + 1)
                    dve.tensor_tensor(buf["W"][d], heads_of(bank[3 * d]), by_head(level[l][:, d, :]), ALU.mult
                                      ).then_inc(g["w"], 1)
                if l in (2, 3):
                    d = l - 2
                    n, c = 2 * T + d, chunk(T % 4, d)
                    dve.wait_ge(g["ks"], n + 1)
                    dve.wait_ge(g["vb"], n + 1)
                    for h in range(HH):
                        last = dve.scalar_tensor_tensor(out=buf["E"][d][:, h, :], in0=bank[6 + d][:, h * P:(h + 1) * P],
                                                        scalar=one("nbeg", c, hf, d, h), in1=buf["E"][d][:, h, :],
                                                        op0=ALU.mult, op1=ALU.add)
                    last.then_inc(g["r"], 1)
            for d in range(DIRS):
                n, c = 2 * T + d, chunk(T % 4, d)
                dve.wait_ge(g["o1"], n + 1)
                dve.wait_ge(g["av"], n + 1)
                dst = hn[:, c, hf * PANEL:(hf + 1) * PANEL]
                dve.tensor_tensor(dst, dst, bank[3 * d + 1][:, :], ALU.add).then_inc(g["o2"], 1)
                dve.wait_ge(g["su"], n + 1)
                for h in range(HH):
                    o_ = slice(h * P, (h + 1) * P)
                    last = dve.scalar_tensor_tensor(out=state[:, d, o_], in0=state[:, d, o_],
                                                    scalar=one("dl", c, hf, d, h), in1=bank[3 * d][:, o_],
                                                    op0=ALU.mult, op1=ALU.add)
                last.then_inc(g["s"], 1)

        block = ctx.enter_context(nc.Block())

        def load_panel(sp, n, src, freed=None):
            if freed:
                sp.wait_ge(*freed)
            sp.dma_start(panel(n), src).then_inc(gu_full[n % RING], 16)

        def moe_sync(sp, l, freed):
            n0 = MOE_AT[l]

            def load(e, i):
                slot = (n0 + i) % RING
                static = isinstance(e, int) and e < RING
                if static:
                    sp.wait_ge(*freed[i])
                else:
                    sp.wait_ge(s["up"], e - RING + 1 + l * PER["up"])
                part = "e (p c) f -> e p (c f)"
                for at, full, name in ((0, gu_full, "moe_w_gate"), (KC * F, up_full, "moe_w_up")):
                    src = ap[name][l].rearrange(part, c=KC)[bass.ds(e, 1)].squeeze(0)
                    sp.dma_start(ring[:, slot, at:at + KC * F], src).then_inc(full[slot], 16)
                if not static:
                    sp.wait_ge(s["y_sum"], 2 * (e - RING) + 2 + l * PER["y_sum"])
                elif l:
                    sp.wait_ge(s["y_sum"], 2 * EXPERTS)
                src = ap["moe_w_down"][l].rearrange(part, c=FC)[bass.ds(e, 1)].squeeze(0)
                sp.dma_start(ring[:, slot, 2 * KC * F:SLOT], src).then_inc(dn_full[slot], 16)

            for e in range(RING):
                load(e, e)
            with sp.Fori(1, 10) as k:
                for i in range(RING):
                    load(k * RING + i, i)
            for e in (30, 31):
                load(e, e % RING)

            def late(e, j, after):
                after()
                part = "e (p c) f -> e p (c f)"
                for at, k, name in ((0, KC, "moe_w_gate"), (KC * F, KC, "moe_w_up"), (2 * KC * F, FC, "moe_w_down")):
                    src = ap[name][l].rearrange(part, c=k)[bass.ds(e, 1)].squeeze(0)
                    sp.dma_start(ring[:, 0, at:at + src.shape[1]], src).then_inc(late_weights[l], 16)

            late_passes(sp, l, None, late)

        def load_constants(sp):
            sp.dma_start(gain[:, 1, :], ap["norm_ffn"][0:1, :].to_broadcast([P, D])).then_inc(gain_in[1], 16)
            sp.dma_start(sink, ap["attn_sink"].to_broadcast([P, A_HEADS])).then_inc(const_in, 16)
            for w, name in enumerate(("attn_q_gain", "attn_k_gain")):
                for two in range(2):
                    sp.dma_start(qk_gain[two * A_DH:(two + 1) * A_DH, w:w + 1],
                                  ap[name].rearrange("a d -> d a")).then_inc(const_in, 16)
            for l in range(2):
                sp.dma_start(router[:, l, :, 0:GROUPS], rows(ap["moe_w_group"][l])).then_inc(const_in, 16)
                sp.dma_start(router[:, l, :, GROUPS:], rows(ap["moe_w_expert"][l])).then_inc(const_in, 16)
                sp.dma_start(router_b[:, l, 0:GROUPS], ap["moe_b_group"][l:l + 1, :].to_broadcast([P, GROUPS])
                              ).then_inc(const_in, 16)
                sp.dma_start(router_b[:, l, GROUPS:], ap["moe_b_expert"][l:l + 1, :].to_broadcast([P, EXPERTS])
                              ).then_inc(const_in, 16)

        @block.sync
        def _(sp):
            for t in range(TT):
                sp.dma_start(x[:, t, :], ap["x"][0, t * P:(t + 1) * P, :]).then_inc(x_in[t], 16)
            for i, j in enumerate(IN_ORDER):
                load_panel(sp, i, rows(ap["attn_w_in"][0])[:, :, j * PANEL:(j + 1) * PANEL],
                           (a["proj"], 4) if i == 2 else None)
                if i == 1:
                    load_constants(sp)
            for j in range(2):
                load_panel(sp, 3 + j, rows(ap["attn_w_out"][0])[:, :, j * PANEL:(j + 1) * PANEL],
                           (a["proj"], 4 * j + 8))
            moe_sync(sp, 0, [(back, 7), (back, 8), (back, 8)])
            w_in, w_out = rows(ap["gdn_w_in"][0]), rows(ap["gdn_w_out"][0])
            sp.wait_ge(s["up"], 30)
            used = [(s["y_sum"], 2 * 30), (s["up"], 32)] + [(g["proj"], 4 * i + 4) for i in range(4)]
            for i in range(6):
                at = (i % 3) * D + (i // 3) * PANEL
                load_panel(sp, GB + i, w_in[:, :, at:at + PANEL], used[i])
            for i in range(2):
                at = 3 * D + i * PANEL
                load_panel(sp, GB + 6 + i, w_in[:, :, at:at + PANEL], (g["proj"], 20 + 4 * i))
            for i in range(2):
                load_panel(sp, GB + 8 + i, w_out[:, :, i * PANEL:(i + 1) * PANEL],
                           (g["zp"], 4 * i + 4))
            moe_sync(sp, 1, [(back, 15), (back, 16), (back, 16)])
            for t in range(TT):
                sp.wait_ge(s["combined"], TT + t + 1)
                sp.dma_start(out[0, t * P:(t + 1) * P, :], x[:, t, :]).then_inc(stored_out, 16)
            sp.wait_ge(stored_out, 16 * TT)

        @block.gpsimd
        def _(pool):
            o = Order(pool, chain["pool"])
            pool.memset(ident[:, :], 0.0)
            pool.memset(mhalf[:, :], -0.5)
            pool.memset(upper[:, :], 1.0)
            pool.memset(ones[:, :], 1.0)
            pool.iota(dist, [[-1, BAND]], base=P, channel_multiplier=1, allow_small_or_imprecise_dtypes=True)
            last = pool.memset(nobody[:, :], NOBODY)
            o.step(last)
            pool.affine_select(out=ident[:, :], in_=ident[:, :], compare_op=ALU.not_equal, fill=1.0, base=0,
                               pattern=[[-1, P]], channel_multiplier=1).then_inc(consts, 1)
            pool.affine_select(out=upper[:, :], in_=upper[:, :], compare_op=ALU.is_gt, fill=0.0, base=0,
                               pattern=[[1, P]], channel_multiplier=-1).then_inc(consts, 1)
            for l in range(2):
                pool.dma_start(tables[l].rearrange("(p r) w -> p (r w)", p=P), nobody[:, :]).then_inc(table_clear, 16)
            norm_pool(pool, 0)
            pool.wait_ge(chain["dve"], 1)
            o.step(pool.affine_select(out=dist, in_=dist, compare_op=ALU.is_ge, fill=FAR, base=0,
                                      pattern=[[1, BAND]], channel_multiplier=-1))
            o.step(pool.affine_select(out=dist, in_=dist, compare_op=ALU.is_ge, fill=FAR, base=2 * P,
                                      pattern=[[-1, BAND]], channel_multiplier=1))
            attention_pool(pool)
            norm_pool(pool, 1)
            moe_pool(pool, 0, o)
            split_low(pool, GB)
            norm_pool(pool, 2)
            gdn_pool(pool, o)
            norm_pool(pool, 3)
            moe_pool(pool, 1, o)

        @block.scalar
        def _(act):
            act.dma_start(gain[:, 0, :], ap["norm_mix"][0:1, :].to_broadcast([P, D])).then_inc(gain_in[0], 16)
            norm_act(act, 0, lambda e, t: e.wait_ge(x_in[t], 16))
            turn_act(act, 0)
            split_high(act, 0)
            act.wait_ge(const_in, 16 * 13)
            attention_act(act)
            act.wait_ge(a["heads"], A_HEADS)
            act.dma_start(gain2, ap["norm_mix"][1:2, :].to_broadcast([P, D])).then_inc(gain_in[2], 16)
            loads_gdn(act)
            turn_act(act, 1)
            norm_act(act, 1, lambda e, t: e.wait_ge(x_half, 2 * t + 2))
            turn_act(act, 2)
            moe_act(act, 0)
            act.wait_ge(s["y_sum"], 2 * EXPERTS)
            split_high(act, GB)
            norm_act(act, 2, lambda e, t: e.wait_ge(s["combined"], t + 1))
            turn_act(act, 3)
            gdn_act(act)
            act.wait_ge(g["zp"], 8)
            act.dma_start(gain[:, 0, :], ap["norm_ffn"][1:2, :].to_broadcast([P, D])).then_inc(gain_in[3], 16)
            turn_act(act, 4)
            split_high(act, GB + 9)
            norm_act(act, 3, lambda e, t: e.wait_ge(x_half, 2 * TT + 2 * t + 2))
            turn_act(act, 5)
            moe_act(act, 1)

        @block.tensor
        def _(pe):
            pe.wait_ge(consts, 2)
            turn_pe(pe, 0, lambda e, t: e.wait_ge(ln["rows"], TT * 0 + t + 1))
            attention_pe(pe)
            turn_pe(pe, 1, lambda e, t: e.wait_ge(a["heads"], A_HEADS))
            project_back_pe(pe, 0, 3, 1)
            turn_pe(pe, 2, lambda e, t: e.wait_ge(ln["rows"], TT * 1 + t + 1))
            moe_pe(pe, 0)
            turn_pe(pe, 3, lambda e, t: e.wait_ge(ln["rows"], 2 * TT + t + 1))
            gdn_pe(pe)
            turn_pe(pe, 4, lambda e, t: e.wait_ge(g["ready"], t + 1))
            project_back_pe(pe, 1, GB + 8, 4)
            turn_pe(pe, 5, lambda e, t: e.wait_ge(ln["rows"], 3 * TT + t + 1))
            moe_pe(pe, 1)

        @block.vector
        def _(dve):
            o = Order(dve, chain["dve"])
            dve.wait_ge(chain["pool"], 1)
            norm_dve(dve, 0)
            split_low(dve, 0)
            dve.wait_ge(const_in, 16 * 13)
            attention_dve(dve, o)
            for t in range(TT):
                turn_dve_one(dve, 1, t)
            project_back_dve(dve, 0)
            norm_dve(dve, 1)
            moe_dve(dve, 0, o)
            norm_dve(dve, 2)
            gdn_dve(dve, o)
            for t in range(TT):
                turn_dve_one(dve, 4, t)
            split_low(dve, GB + 9)
            project_back_dve(dve, 1)
            norm_dve(dve, 3)
            moe_dve(dve, 1, o)


_OUT = ((1, SEQ, D), "float32")


def kernel(**inputs):
    import concourse.bacc as bacc
    from concourse.bass_utils import run_bass_kernel_spmd

    nc = bacc.Bacc("TRN2", target_bir_lowering=False, num_devices=1)
    arrays, aps = {}, {}
    for name, value in inputs.items():
        value = np.ascontiguousarray(value)
        arrays["in_" + name] = value
        aps[name] = nc.dram_tensor("in_" + name, value.shape, mybir.dt.from_np(value.dtype),
                                   kind="ExternalInput").ap()
    out = nc.dram_tensor("out_0", _OUT[0], F32, kind="ExternalOutput").ap()
    build(nc, aps, out)
    done = run_bass_kernel_spmd(nc, [arrays], core_ids=[0])
    return done.results[0]["out_0"]
```
